# Optimizing a Trainium2 kernel written in Bass

```python
import math
import jax, jax.numpy as jnp
from jax import lax
import numpy as np

D_MODEL = 1024
BATCH = 1
SEQ = 512
DEPTH = 2
DEC_BATCH = 1
DEC_SEQ = 32
PAST_LEN = 256

CHUNK = 64
PLE_DIM = 256
EPS = 1e-6
GM_CHUNK = 128
GM_GROUPS = 8
GM_DIM = D_MODEL
GM_GDIM = GM_DIM // GM_GROUPS
SSM_HEADS = 16
SSM_HEAD_DIM = 64
SSM_DIM = SSM_HEADS * SSM_HEAD_DIM
SSM_GROUPS = 2
SSM_STATE = 128
SSM_CONV = 4
SSM_CONV_DIM = SSM_DIM + 2 * SSM_GROUPS * SSM_STATE
RET_HEADS = 8
RET_DK = 128
RET_DV = 256
RET_QK = RET_HEADS * RET_DK
RET_V = RET_HEADS * RET_DV
ROPE_BASE = 10000.0
D_FF = 2816
FFN_CONV = 3
IN0 = 2 * GM_DIM + SSM_DIM + SSM_CONV_DIM + SSM_HEADS
MIX0 = GM_DIM + SSM_DIM
IN1 = 2 * RET_QK + 2 * RET_V
SPLIT0 = (GM_DIM, 2 * GM_DIM, 2 * GM_DIM + SSM_DIM, 2 * GM_DIM + SSM_DIM + SSM_CONV_DIM)
SPLIT1 = (RET_QK, 2 * RET_QK, 2 * RET_QK + RET_V)

kernel_name = 'chunk_causal_gmlp_ssd_retention_convffn_step'

def rmsnorm(x, g):
    xf = x.astype(jnp.float32)
    y = xf * lax.rsqrt(jnp.mean(xf * xf, axis=-1, keepdims=True) + EPS)
    return (y * g.astype(jnp.float32)).astype(x.dtype)

def causal_dwconv(x, buf, w, b):
    width = w.shape[0]
    length = x.shape[1]
    xp = jnp.concatenate([buf.astype(x.dtype), x], axis=1)
    y = b.astype(x.dtype)
    for k in range(width):
        y = y + w[k] * xp[:, k:k + length]
    return y, xp[:, length:]

def gmlp_mix(u, v, v_gain, w_s, b_s):
    bsz, length, _ = u.shape
    n = min(length, GM_CHUNK)
    u = jax.nn.gelu(u)
    v = rmsnorm(jax.nn.gelu(v).reshape(bsz, length, GM_GROUPS, GM_GDIM), v_gain.reshape(GM_GROUPS, GM_GDIM))
    pos = jnp.arange(n)
    mask = (pos[None, :] // CHUNK) <= (pos[:, None] // CHUNK)
    w = jnp.where(mask[None], w_s[:, :n, :n], 0.0).astype(v.dtype)
    vc = v.reshape(bsz, length // n, n, GM_GROUPS, GM_GDIM)
    s = jnp.einsum('gij,bcjgd->bcigd', w, vc) + b_s[:, :n].T[None, None, :, :, None].astype(v.dtype)
    return u * s.reshape(bsz, length, GM_DIM), v.reshape(bsz, length, GM_DIM)

def ssd_scan(x, dt, a, bm, cm, h0):
    f32 = jnp.float32
    bsz, length = x.shape[:2]
    t_len = min(length, CHUNK)
    nc = length // t_len
    r = SSM_HEADS // SSM_GROUPS
    xs = (x * dt[..., None]).astype(f32).reshape(bsz, nc, t_len, SSM_GROUPS, r, SSM_HEAD_DIM)
    da = (dt.astype(f32) * a.astype(f32)).reshape(bsz, nc, t_len, SSM_GROUPS, r)
    bc = bm.astype(f32).reshape(bsz, nc, t_len, SSM_GROUPS, SSM_STATE)
    cc = cm.astype(f32).reshape(bsz, nc, t_len, SSM_GROUPS, SSM_STATE)
    cs = jnp.cumsum(da, axis=2)
    tril = jnp.tril(jnp.ones((t_len, t_len), bool))[None, None, :, :, None, None]
    seg = cs[:, :, :, None] - cs[:, :, None, :]
    lmat = jnp.exp(jnp.where(tril, seg, -jnp.inf))
    cb = jnp.einsum('bctgn,bcsgn->bctsg', cc, bc)
    y_diag = jnp.einsum('bctsg,bctsgr,bcsgrp->bctgrp', cb, lmat, xs)
    decay_to_end = jnp.exp(cs[:, :, -1:] - cs)
    chunk_states = jnp.einsum('bctgn,bctgr,bctgrp->bcgrpn', bc, decay_to_end, xs)
    chunk_decay = jnp.exp(cs[:, :, -1])

    def step(h, inp):
        st, dec = inp
        return h * dec[..., None, None] + st, h

    h_init = h0.astype(f32).reshape(bsz, SSM_GROUPS, r, SSM_HEAD_DIM, SSM_STATE)
    h_last, h_prev = lax.scan(step, h_init, (jnp.moveaxis(chunk_states, 1, 0), jnp.moveaxis(chunk_decay, 1, 0)))
    h_prev = jnp.moveaxis(h_prev, 0, 1)
    y_off = jnp.einsum('bctgn,bcgrpn,bctgr->bctgrp', cc, h_prev, jnp.exp(cs))
    y = (y_diag + y_off).reshape(bsz, length, SSM_HEADS, SSM_HEAD_DIM)
    return y, h_last.reshape(bsz, SSM_HEADS, SSM_HEAD_DIM, SSM_STATE).astype(h0.dtype)

def mamba_mix(z, xbc, dt_raw, conv_buf, h0, conv_w, conv_b, dt_bias, a_log, d_skip, norm_g):
    bsz, length = z.shape[:2]
    xbc, new_buf = causal_dwconv(xbc, conv_buf, conv_w, conv_b)
    xbc = jax.nn.silu(xbc)
    xh, bm, cm = jnp.split(xbc, [SSM_DIM, SSM_DIM + SSM_GROUPS * SSM_STATE], axis=-1)
    xh = xh.reshape(bsz, length, SSM_HEADS, SSM_HEAD_DIM)
    bm = bm.reshape(bsz, length, SSM_GROUPS, SSM_STATE)
    cm = cm.reshape(bsz, length, SSM_GROUPS, SSM_STATE)
    dt = jax.nn.softplus((dt_raw + dt_bias).astype(jnp.float32))
    a = -jnp.exp(a_log.astype(jnp.float32))
    y, h_last = ssd_scan(xh, dt, a, bm, cm, h0)
    y = (y + d_skip.astype(jnp.float32)[:, None] * xh.astype(jnp.float32)).reshape(bsz, length, SSM_DIM).astype(z.dtype)
    y = rmsnorm(y * jax.nn.silu(z), norm_g)
    return y, new_buf, h_last

def rope(x, pos):
    half = x.shape[-1] // 2
    inv = ROPE_BASE ** (-jnp.arange(half, dtype=jnp.float32) / half)
    ang = pos.astype(jnp.float32)[:, None] * inv[None]
    cos = jnp.cos(ang)[None, :, None, :]
    sin = jnp.sin(ang)[None, :, None, :]
    xf = x.astype(jnp.float32)
    x1, x2 = xf[..., :half], xf[..., half:]
    return jnp.concatenate([x1 * cos - x2 * sin, x1 * sin + x2 * cos], axis=-1)

def retention(q, k, v, s0):
    f32 = jnp.float32
    bsz, length = q.shape[:2]
    t_len = min(length, CHUNK)
    nc = length // t_len
    lg = jnp.log(1.0 - 2.0 ** (-5.0 - jnp.arange(RET_HEADS, dtype=f32)))
    qc = q.reshape(bsz, nc, t_len, RET_HEADS, RET_DK)
    kc = k.reshape(bsz, nc, t_len, RET_HEADS, RET_DK)
    vc = v.astype(f32).reshape(bsz, nc, t_len, RET_HEADS, RET_DV)
    t = jnp.arange(t_len, dtype=f32)
    diff = t[:, None] - t[None, :]
    dmat = jnp.where(diff[None] >= 0, jnp.exp(lg[:, None, None] * jnp.maximum(diff, 0.0)[None]), 0.0)
    scores = jnp.einsum('bcthd,bcshd->bchts', qc, kc) * dmat[None, None]
    y_intra = jnp.einsum('bchts,bcshe->bcthe', scores, vc)
    q_decay = jnp.exp(lg[None, :] * (t[:, None] + 1.0))
    k_decay = jnp.exp(lg[None, :] * (t_len - 1.0 - t)[:, None])
    chunk_kv = jnp.einsum('bcthd,th,bcthe->bchde', kc, k_decay, vc)
    chunk_decay = jnp.exp(lg * t_len)

    def step(s, kv):
        return s * chunk_decay[None, :, None, None] + kv, s

    s_last, s_prev = lax.scan(step, s0.astype(f32), jnp.moveaxis(chunk_kv, 1, 0))
    s_prev = jnp.moveaxis(s_prev, 0, 1)
    y_inter = jnp.einsum('bcthd,bchde,th->bcthe', qc, s_prev, q_decay)
    y = (y_intra + y_inter).reshape(bsz, length, RET_HEADS, RET_DV)
    return y, s_last.astype(s0.dtype)

def head_norm(y, g):
    mu = jnp.mean(y, axis=-1, keepdims=True)
    var = jnp.mean(jnp.square(y - mu), axis=-1, keepdims=True)
    yn = (y - mu) * lax.rsqrt(var + EPS)
    return yn.reshape(y.shape[0], y.shape[1], RET_V) * g.astype(jnp.float32)

def retention_mix(h, s0, pos, w_in, w_out, norm_g):
    bsz, length = h.shape[:2]
    proj = h @ w_in
    q, k, v, g = jnp.split(proj, SPLIT1, axis=-1)
    q = rope(q.reshape(bsz, length, RET_HEADS, RET_DK), pos)
    k = rope(k.reshape(bsz, length, RET_HEADS, RET_DK), pos) * (RET_DK ** -0.5)
    v = v.reshape(bsz, length, RET_HEADS, RET_DV)
    y, s_last = retention(q, k, v, s0)
    y = head_norm(y, norm_g).astype(h.dtype)
    return (jax.nn.silu(g) * y) @ w_out, s_last

def conv_ffn(h, buf, w_gate, w_up, conv_w, conv_b, w_down):
    g = h @ w_gate
    u = h @ w_up
    g, new_buf = causal_dwconv(g, buf, conv_w, conv_b)
    return (jax.nn.silu(g) * u) @ w_down, new_buf

def trunk(x, p, ssm_conv_buf, ssm_h, ret_s, ffn_bufs, pos0, weights):
    (norm_mix, norm_ffn, norm_ple, norm_final, l0_w_in, gm_v_gain, gm_w_s, gm_b_s,
     ssm_conv_w, ssm_conv_b, ssm_dt_bias, ssm_a_log, ssm_d, ssm_norm, l0_w_out,
     l1_w_in, ret_norm, l1_w_out, ffn_w_gate, ffn_w_up, ffn_conv_w, ffn_conv_b,
     ffn_w_down, ple_w_gate, ple_w_proj) = weights
    length = x.shape[1]
    pos = pos0 + jnp.arange(length)
    new_ffn = []
    for i in range(DEPTH):
        h = rmsnorm(x, norm_mix[i])
        if i % 2 == 0:
            proj = h @ l0_w_in
            u, v, z, xbc, dt_raw = jnp.split(proj, SPLIT0, axis=-1)
            ya, gm_v = gmlp_mix(u, v, gm_v_gain, gm_w_s, gm_b_s)
            yb, ssm_conv_buf, ssm_h = mamba_mix(z, xbc, dt_raw, ssm_conv_buf, ssm_h, ssm_conv_w, ssm_conv_b,
                                                ssm_dt_bias, ssm_a_log, ssm_d, ssm_norm)
            x = x + jnp.concatenate([ya, yb], axis=-1) @ l0_w_out
        else:
            yc, ret_s = retention_mix(h, ret_s, pos, l1_w_in, l1_w_out, ret_norm)
            x = x + yc
        h = rmsnorm(x, norm_ffn[i])
        yf, fb = conv_ffn(h, ffn_bufs[i], ffn_w_gate[i], ffn_w_up[i], ffn_conv_w[i], ffn_conv_b[i], ffn_w_down[i])
        new_ffn.append(fb)
        x = x + yf
        gate = jax.nn.sigmoid(rmsnorm(x, norm_ple[i]) @ ple_w_gate[i])
        x = x + gate * (p[i] @ ple_w_proj[i])
    x = rmsnorm(x, norm_final)
    return x, gm_v, ssm_conv_buf, ssm_h, ret_s, jnp.stack(new_ffn)

def setup_inputs(seed: int = 0) -> dict:
    key = jax.random.key(seed)
    keys = iter(jax.random.split(key, 48))
    f32 = jnp.float32

    def nrm(shape, scale):
        return jax.random.normal(next(keys), shape, f32) * scale

    def gain(shape):
        return 1.0 + 0.02 * jax.random.normal(next(keys), shape, f32)

    dt0 = jnp.exp(jax.random.uniform(next(keys), (SSM_HEADS,), f32, math.log(1e-3), math.log(1e-1)))
    return {
        'x_prompt': nrm((BATCH, SEQ, D_MODEL), 1.0),
        'x_sample': nrm((DEC_BATCH, DEC_SEQ, D_MODEL), 1.0),
        'state_ssm_conv': nrm((DEC_BATCH, SSM_CONV - 1, SSM_CONV_DIM), 1.0),
        'state_ssm': nrm((DEC_BATCH, SSM_HEADS, SSM_HEAD_DIM, SSM_STATE), 0.1),
        'state_ret': nrm((DEC_BATCH, RET_HEADS, RET_DK, RET_DV), 0.1),
        'state_ffn_conv': nrm((DEPTH, DEC_BATCH, FFN_CONV - 1, D_FF), 1.0),
        'p_prompt': nrm((DEPTH, BATCH, SEQ, PLE_DIM), 1.0),
        'p_sample': nrm((DEPTH, DEC_BATCH, DEC_SEQ, PLE_DIM), 1.0),
        'norm_mix': gain((DEPTH, D_MODEL)),
        'norm_ffn': gain((DEPTH, D_MODEL)),
        'norm_ple': gain((DEPTH, D_MODEL)),
        'norm_final': gain((D_MODEL,)),
        'l0_w_in': nrm((D_MODEL, IN0), D_MODEL ** -0.5),
        'gm_v_gain': gain((GM_DIM,)),
        'gm_w_s': nrm((GM_GROUPS, GM_CHUNK, GM_CHUNK), GM_CHUNK ** -0.5),
        'gm_b_s': gain((GM_GROUPS, GM_CHUNK)),
        'ssm_conv_w': nrm((SSM_CONV, SSM_CONV_DIM), SSM_CONV ** -0.5),
        'ssm_conv_b': nrm((SSM_CONV_DIM,), 0.02),
        'ssm_dt_bias': dt0 + jnp.log(-jnp.expm1(-dt0)),
        'ssm_a_log': jnp.log(jax.random.uniform(next(keys), (SSM_HEADS,), f32, 1.0, 16.0)),
        'ssm_d': gain((SSM_HEADS,)),
        'ssm_norm': gain((SSM_DIM,)),
        'l0_w_out': nrm((MIX0, D_MODEL), MIX0 ** -0.5),
        'l1_w_in': nrm((D_MODEL, IN1), D_MODEL ** -0.5),
        'ret_norm': gain((RET_V,)),
        'l1_w_out': nrm((RET_V, D_MODEL), RET_V ** -0.5),
        'ffn_w_gate': nrm((DEPTH, D_MODEL, D_FF), D_MODEL ** -0.5),
        'ffn_w_up': nrm((DEPTH, D_MODEL, D_FF), D_MODEL ** -0.5),
        'ffn_conv_w': nrm((DEPTH, FFN_CONV, D_FF), FFN_CONV ** -0.5),
        'ffn_conv_b': nrm((DEPTH, D_FF), 0.02),
        'ffn_w_down': nrm((DEPTH, D_FF, D_MODEL), D_FF ** -0.5),
        'ple_w_gate': nrm((DEPTH, D_MODEL, D_MODEL), D_MODEL ** -0.5),
        'ple_w_proj': nrm((DEPTH, PLE_DIM, D_MODEL), PLE_DIM ** -0.5),
    }

def reference(x_prompt, x_sample, state_ssm_conv, state_ssm, state_ret, state_ffn_conv, p_prompt, p_sample,
              norm_mix, norm_ffn, norm_ple, norm_final, l0_w_in, gm_v_gain, gm_w_s, gm_b_s,
              ssm_conv_w, ssm_conv_b, ssm_dt_bias, ssm_a_log, ssm_d, ssm_norm, l0_w_out,
              l1_w_in, ret_norm, l1_w_out, ffn_w_gate, ffn_w_up, ffn_conv_w, ffn_conv_b,
              ffn_w_down, ple_w_gate, ple_w_proj):
    weights = (norm_mix, norm_ffn, norm_ple, norm_final, l0_w_in, gm_v_gain, gm_w_s, gm_b_s,
               ssm_conv_w, ssm_conv_b, ssm_dt_bias, ssm_a_log, ssm_d, ssm_norm, l0_w_out,
               l1_w_in, ret_norm, l1_w_out, ffn_w_gate, ffn_w_up, ffn_conv_w, ffn_conv_b,
               ffn_w_down, ple_w_gate, ple_w_proj)
    bp = x_prompt.shape[0]
    dtp = x_prompt.dtype
    zero_ssm_conv = jnp.zeros((bp, SSM_CONV - 1, SSM_CONV_DIM), dtp)
    zero_ssm = jnp.zeros((bp, SSM_HEADS, SSM_HEAD_DIM, SSM_STATE), state_ssm.dtype)
    zero_ret = jnp.zeros((bp, RET_HEADS, RET_DK, RET_DV), state_ret.dtype)
    zero_ffn = jnp.zeros((DEPTH, bp, FFN_CONV - 1, D_FF), dtp)
    y_prompt, _, ssm_conv_p, ssm_p, ret_p, ffn_p = trunk(
        x_prompt, p_prompt, zero_ssm_conv, zero_ssm, zero_ret, zero_ffn, 0, weights)
    y_sample, gm_v_s, ssm_conv_s, ssm_s, ret_s, ffn_s = trunk(
        x_sample, p_sample, state_ssm_conv, state_ssm, state_ret, state_ffn_conv, PAST_LEN, weights)
    return (y_prompt, y_sample, ssm_conv_p, ssm_conv_s, ssm_p, ssm_s, ret_p, ret_s, ffn_p, ffn_s, gm_v_s)


_drawn_inputs = setup_inputs


def setup_inputs(seed=0):
    import zlib

    import numpy as np

    out = dict(_drawn_inputs(seed))
    spreads = {}
    factors = {'norm_ple': 64.0,
     'norm_final': 8.277,
     'gm_v_gain': 8.204,
     'gm_b_s': 5.669,
     'ssm_d': 15.583,
     'ssm_norm': 3.506,
     'ret_norm': 28.275,
     'ffn_conv_b': 4.93,
     'norm_ffn': 2.737}
    for name, (base, spread) in spreads.items():
        noise = np.random.default_rng([zlib.crc32(name.encode()), seed]).standard_normal(out[name].shape)
        drawn = base * np.exp(spread * noise) if base else spread * noise
        out[name] = __import__('jax').numpy.asarray(drawn.astype(out[name].dtype))
    for name, factor in factors.items():
        out[name] = (out[name] * factor).astype(out[name].dtype)
    return out
```

```python
import numpy as np

P = 128
TP, TS = 512, 32
T = TP + TS
HALF = 256
D = 1024
KD = D // P
D_FF = 2816
FT = D_FF // P
FFN_PARTS = (8, 8, 6)
GROUPS = 8
SH, SP_, SN = 16, 64, 128
XBC = (SH * SP_ + 2 * 2 * SN) // P
RH, RDK, RDV = 8, 128, 256
PAST = 256
CH = 128
NC = TP // CH
EPS = 1e-6
RING = 4

VEC = {}
_at = 0
for _name, _n in (("mix0", KD), ("ffn0", KD), ("ple0", KD), ("mix1", KD), ("ffn1", KD), ("ple1", KD), ("final", KD),
                  ("ssm_w", 4 * XBC), ("ssm_b", XBC), ("fw0", 3 * FT), ("fb0", FT), ("fw1", 3 * FT), ("fb1", FT),
                  ("ssm_norm", KD), ("ret_norm", 2 * RH), ("kdec", RH), ("kdec_s", RH), ("g_chunk", RH), ("g_sample", RH)):
    VEC[_name] = _at
    _at += _n
NVEC = _at


def phase_table():
    t = [("v", 8, 8, 1), ("u", 8, 8, 1), ("xbc", XBC, 8, 1), ("outa", 8, 8, 1), ("z", 8, 8, 1), ("outb", 8, 8, 1)]
    for layer in range(2):
        if layer:
            t += [("heads_a", 30, 8, 1), ("ret_a", 8, 8, 1), ("heads_b", 18, 8, 1), ("ret_b", 8, 8, 1)]
        for part, n in enumerate(FFN_PARTS):
            t += [(f"gu{layer}{part}", 2 * n, 8, 1), (f"down{layer}{part}", KD, n, 1)]
        t += [(f"pp{layer}", 4, 2, 2), (f"gate{layer}", 8, 8, 1)]
    return t


class Phase:
    def __init__(self, name, slabs, kt, m, slab0, group0):
        self.name, self.slabs, self.kt, self.m, self.s0, self.g0 = name, slabs, kt, m, slab0, group0
        self.width = kt * m * P


def phases():
    out, s, g = {}, 0, 0
    for name, n, kt, m in phase_table():
        out[name] = Phase(name, n, kt, m, s, g)
        s, g = s + n, g + n * m
        if name == "xbc":
            g += 1
    return out, s


class At:
    def __init__(self, c, k=0, i=None):
        self.c, self.k, self.i = c, k, i

    def __add__(self, n):
        return At(self.c + n, self.k, self.i)

    def __mul__(self, n):
        return At(self.c * n, self.k * n, self.i)

    def div(self, n):
        assert self.k % n == 0
        return At(self.c // n, self.k // n, self.i)

    def mod(self, n):
        assert self.k % n == 0
        return self.c % n

    @property
    def v(self):
        return self.c if self.i is None or not self.k else self.i * self.k + self.c


def each(eng, count, body, per=4, peel=0, least=3):
    for n in range(peel):
        body(At(n))
    turns = (count - peel) // per
    if turns >= least:
        with eng.Fori(0, turns) as i:
            for j in range(per):
                body(At(peel + j, per, i))
    else:
        turns = 0
    for n in range(peel + turns * per, count):
        body(At(n))


def build(nc, A, O):
    import concourse.bass as bass
    import concourse.mybir as mybir
    from contextlib import ExitStack

    F = mybir.dt.float32
    R = mybir.dt.float32r
    ACT = mybir.ActivationFunctionType
    ALU = mybir.AluOpType
    AX = mybir.AxisListType
    ds = bass.ds
    PH, NSLABS = phases()
    ORDER = [PH[t[0]] for t in phase_table()]

    def phase_of(s):
        for p in ORDER:
            if p.s0 <= s < p.s0 + p.slabs:
                return p
        return None

    def groups_done(s):
        p = phase_of(s)
        return p.g0 + (s - p.s0 + 1) * p.m

    DT_GROUP = PH["xbc"].g0 + XBC

    ctx = ExitStack()
    with ctx:
        def sb(name, cols, dt=F):
            return ctx.enter_context(nc.sbuf_tensor(name, [P, cols], dt))

        sems = {}

        def sem(name):
            if name not in sems:
                sems[name] = ctx.enter_context(nc.semaphore(name))
            return sems[name]

        x = sb("x", KD * T)
        op_hi = [sb(f"op{i}_hi", KD * T, R) for i in range(2)]
        op_lo = [sb(f"op{i}_lo", KD * T, R) for i in range(2)]
        SLAB = 8 * P
        w_raw = sb("w_raw", RING * SLAB)
        w_hi = sb("w_hi", RING * SLAB, R)
        w_lo = sb("w_lo", RING * SLAB, R)
        vec = sb("vec", NVEC)
        rstd = sb("rstd", T)
        ident = sb("ident", P)
        ones = sb("ones", P)
        tri = sb("tri", P)
        neg = sb("neg", P)
        sq = sb("sq", 2 * T)
        ssq = sb("ssq", T)
        eps = sb("eps", 1)
        token = sb("token", 2)
        ffn_state = sb("ffn_state", 2 * FT * 2)
        ffn_tail = sb("ffn_tail", 2 * FT * 4)
        head_rows = sb("head_rows", 3 * SH)
        a_row = sb("a_row", SH)
        conv_state = sb("conv_state", XBC * 3)
        conv_tail = sb("conv_tail", XBC * 6)
        w_dt = sb("w_dt", 8 * SH)
        w_dt_hi = sb("w_dt_hi", 8 * SH, R)
        w_dt_lo = sb("w_dt_lo", 8 * SH, R)
        rstd_root = sq[:, 0:T]
        ARENA = 15200
        arena = sb("arena", ARENA)

        class Region:
            def __init__(self, at=0):
                self.at = at

            def take(self, n):
                v = arena[:, self.at:self.at + n]
                self.at += n
                assert self.at <= ARENA, self.at
                return v

        r = Region()
        v_raw = r.take(KD * T)
        gain_rows, w_spatial, bs_row, v_sq0 = (v_raw[:, i * D:(i + 1) * D] for i in range(4))
        v_tok = r.take((NC + 1) * D)
        u_g = r.take(KD * T)
        v_gelu = r.take(2 * T)
        v_sq = (v_sq0, v_gelu[:, 0:D])
        ms_v = ssq[:, 0:(NC + 1) * GROUPS]
        ya = sq
        r = Region()
        xbc = r.take(XBC * T)
        temps = r.at
        xpad = r.take(2 * (T + 6))
        conv = r.take(2 * (T + 3))
        dt_t = r.take(T)
        r = Region(temps)
        x_tok, bc_tok, xs, xsd, y_tok, mix = (r.take(n) for n in (D, 512, D, D, D, 2 * 512))
        z_buf = arena[:, temps:temps + 2 * T]
        s_prompt, s_sample = r.take(D), r.take(D)
        NP_ = (NC + 1) * SH
        (dt_b, da, cs, ecs, dte, etot, p_a, p_b, p_c, p_d) = (r.take(NP_) for _ in range(10))
        r = Region()
        gpad = r.take(2 * (T + 4))
        facc = r.take(2 * (T + 2))
        fsg = r.take(2 * T)
        fsgr = r.take(2 * T)
        hid = r.take(2 * T)
        p_proj = r.take(KD * T)
        p_raw = p_proj[:, 0:2 * T]
        gate_t = r.take(2 * T)
        TABLES = r.at
        cos_q, sin_q, cos_k, sin_k = (r.take(T) for _ in range(4))
        dmat = r.take(RH * CH)
        qdec = r.take(RH * CH)
        r = Region()
        k_t, q_t, qd, rot, rot_sw = (r.take(T) for _ in range(5))
        v_t, g_s = r.take(2 * T), r.take(2 * T)
        k_tok = r.take((NC + 1) * RDK)
        rv_tok = r.take((NC + 1) * RDV)
        sc = r.take(NC * CH + TS)
        s_hist = r.take(NC * RDV)
        s_in, s_out = r.take(RDV), r.take(RDV)
        yn = r.take((NC + 1) * RDV)
        stats, mv, sd = r.take((NC + 1) * 6), r.take((NC + 1) * 2), r.take(NC + 1)
        assert r.at <= TABLES

        proj = ctx.enter_context(nc.psum_tensor("proj", [P, 4, 512], F))
        Q = ctx.enter_context(nc.psum_tensor("Q", [P, 4, 512], F))

        w_loaded = [sem(f"w_loaded{i}") for i in range(RING)]
        w_hi_done, w_lo_done = sem("w_hi_done"), sem("w_lo_done")
        tile_done = sem("tile_done")
        tile_read = sem("tile_read")
        consts_in = sem("consts_in")
        stored = sem("stored")

        def part(buf, n, lo, size, pitch=T):
            if isinstance(n, int):
                return buf[:, n * pitch + lo:n * pitch + lo + size]
            return buf[:, ds((n * pitch + lo).v, size)]

        def col(table, n):
            return vec[:, ds((n + VEC[table]).v, 1)] if not isinstance(n, int) else vec[:, VEC[table] + n:VEC[table] + n + 1]

        def two(ap):
            return ap.rearrange("p (a b) -> p a b", a=2)

        def four(ap):
            return ap.rearrange("p (a b) -> p a b", a=4)

        def out_prompt(g, rows=P):
            q = g.mod(2)
            return proj[0:rows, 2 * q:2 * q + 2, 0:HALF]

        def out_sample(g, rows=P):
            return proj[0:rows, 2 * g.mod(2) + 1, HALF:HALF + TS]

        NORMS = ("n_in", "n_yb", "n_ffn0", "n_ple0", "n_mix1", "n_ffn1", "n_ple1", "n_out")
        RISES = {"hi": KD, "lo": KD, "sq": KD, "ssq": KD, "zero": 1, "ms": 1, "root": 1, "rstd": 1}

        def nsem(kind):
            return sem("norm_" + kind)

        def ncount(name, kind, n):
            before = NORMS.index(name) * RISES[kind]
            return (n + before).v if isinstance(n, At) else n + before

        def slab(pe, ph, n, ops, ready=None, k0=0):
            s = n + ph.s0
            slot = s.mod(RING)
            pe.wait_ge(w_lo_done, (s + 1).v)
            for m in range(ph.m):
                g = (n * ph.m) + (ph.g0 + m)
                if g.k or g.c >= 2:
                    pe.wait_ge(tile_read, (g + -1).v)
                for k in range(ph.kt):
                    if ready:
                        pe.wait_ge(ready[0], ready[1] + k)
                    lo = slot * SLAB + (k * ph.m + m) * P
                    passes = ((w_hi, op_hi[ops]), (w_hi, op_lo[ops]), (w_lo, op_hi[ops]))
                    for j, (w, o) in enumerate(passes):
                        for half in range(2):
                            size = HALF if half == 0 else HALF + TS
                            at = (k0 + k) * T + half * HALF
                            last = nc.tensor.matmul(proj[:, 2 * g.mod(2) + half, 0:size], w[:, lo:lo + P],
                                                    o[:, at:at + size], start=(k == 0 and j == 0),
                                                    stop=(k == ph.kt - 1 and j == 2))
                last.then_inc(tile_done, 1)

        def mean_square(pe, name, free=()):
            pe.wait_ge(nsem("ssq"), ncount(name, "ssq", KD))
            for s_, v_ in free:
                pe.wait_ge(s_, v_)
            nc.tensor.matmul(Q[:, 2, 0:HALF], ones[:, :], ssq[:, 0:HALF], start=True, stop=True)
            nc.tensor.matmul(Q[:, 3, 0:HALF + TS], ones[:, :], ssq[:, HALF:T], start=True, stop=True)\
                .then_inc(nsem("ms"), 1)

        def split_high(act, s):
            width = phase_of(s.c).width
            slot = s.mod(RING)
            act.wait_ge(w_loaded[slot], (s.div(RING) * 16 + 16).v)
            c = slot * SLAB
            nc.scalar.activation(w_hi[:, c:c + width], w_raw[:, c:c + width], ACT.Copy).then_inc(w_hi_done, 1)

        def split_ahead(act, ph, n):
            s = n + ph.s0
            if not n.k and s.c + RING >= NSLABS:
                return
            g = (n * ph.m) + (ph.g0 + ph.m)
            act.wait_ge(tile_done, g.v)
            split_high(act, s + RING)

        def each_ahead(act, ph, body, per=4, peel=0):
            nxt = phase_of(ph.s0 + ph.slabs)
            if nxt is not None and nxt.width == ph.width:
                each(act, ph.slabs, body, per, peel)
            else:
                each(act, ph.slabs - RING, body, per, peel)
                for n in range(ph.slabs - RING, ph.slabs):
                    body(At(n))

        def act_root(act, name):
            act.wait_ge(nsem("ms"), ncount(name, "ms", 1))
            nc.scalar.activation(rstd_root[:, 0:HALF], Q[:, 2, 0:HALF], ACT.Sqrt, bias=eps[:, 0:1], scale=1.0 / D)
            nc.scalar.activation(rstd_root[:, HALF:T], Q[:, 3, 0:HALF + TS], ACT.Sqrt, bias=eps[:, 0:1],
                                 scale=1.0 / D).then_inc(nsem("root"), 1)

        def dve_rstd(dve, name):
            dve.wait_ge(nsem("root"), ncount(name, "root", 1))
            nc.vector.reciprocal(rstd[:, :], rstd_root[:, :]).then_inc(nsem("rstd"), 1)
            dve.wait_ge(nsem("rstd"), ncount(name, "rstd", 1))

        def act_operand(act, name, n, src):
            gain, ops = NORM[name]
            nc.scalar.activation(part(op_hi[ops], n, 0, T), src, ACT.Copy, scale=col(gain, n))\
                .then_inc(nsem("hi"), 1)
            act_square(act, name, n, src)

        def act_square(act, name, n, src):
            q = n.mod(2)
            if n.k or n.c >= 2:
                act.wait_ge(nsem("ssq"), ncount(name, "ssq", n + -1))
            nc.scalar.activation(sq[:, q * T:(q + 1) * T], src, ACT.Square).then_inc(nsem("sq"), 1)

        def dve_operand(dve, name, n, src):
            gain, ops = NORM[name]
            dve.wait_ge(nsem("hi"), ncount(name, "hi", n + 1))
            nc.vector.scalar_tensor_tensor(out=part(op_lo[ops], n, 0, T), in0=src, scalar=col(gain, n),
                                           in1=part(op_hi[ops], n, 0, T), op0=ALU.mult, op1=ALU.subtract)\
                .then_inc(nsem("lo"), 1)

        def pool_squares(pool, name, before):
            if before:
                pool.wait_ge(nsem("ms"), ncount(before, "ms", 1))
            nc.gpsimd.memset(ssq[:, :], 0.0).then_inc(nsem("zero"), 1)
            pool.wait_ge(nsem("zero"), ncount(name, "zero", 1))

        def pool_square(pool, name, n):
            q = n.mod(2)
            pool.wait_ge(nsem("sq"), ncount(name, "sq", n + 1))
            if n.k or n.c >= 1:
                pool.wait_ge(nsem("ssq"), ncount(name, "ssq", n))
            nc.gpsimd.tensor_tensor(ssq[:, :], ssq[:, :], sq[:, q * T:(q + 1) * T], ALU.add)\
                .then_inc(nsem("ssq"), 1)

        def split_low(pool, s):
            width = phase_of(s.c).width
            c = s.mod(RING) * SLAB
            pool.wait_ge(w_hi_done, (s + 1).v)
            nc.gpsimd.tensor_tensor(w_lo[:, c:c + width], w_raw[:, c:c + width], w_hi[:, c:c + width],
                                    ALU.subtract).then_inc(w_lo_done, 1)

        def low_ahead(pool, ph, n):
            s = n + (ph.s0 + RING)
            if n.k or s.c < NSLABS:
                split_low(pool, s)

        block = ctx.enter_context(nc.Block())

        NORM = {"n_in": ("mix0", 0), "n_yb": ("ssm_norm", 0), "n_ffn0": ("ffn0", 1), "n_ple0": ("ple0", 1),
                "n_mix1": ("mix1", 0), "n_ffn1": ("ffn1", 0), "n_ple1": ("ple1", 0)}
        HID = (0, 1)
        LAYER = ("n_ffn0", "n_ffn1")
        PLE = ("n_ple0", "n_ple1")

        N_CONSTS = 7

        def heads(eng, head, between, drain=None):
            head("heads_a", At(0), 0)
            with eng.Fori(0, 2) as i:
                head("heads_a", At(1, 2, i), 0)
                head("heads_a", At(2, 2, i), 0)
            between()
            for h in (5, 6, 7):
                head("heads_b", At(h), 5)
            if drain:
                drain()

        @block.sync
        def _(sp):
            def load(dst, src):
                sp.dma_start(dst, src).then_inc(consts_in, 16)

            def weights(name):
                ph = PH[name]

                def one(n):
                    s = n + ph.s0
                    slot = s.mod(RING)
                    if s.k or s.c >= RING:
                        sp.wait_ge(w_lo_done, (s + (1 - RING)).v)
                    src = A["w_" + ph.name][ds(n.v, 1), :, :] if n.k else A["w_" + ph.name][n.c:n.c + 1, :, :]
                    sp.dma_start(w_raw[:, slot * SLAB:slot * SLAB + ph.width],
                                 src.rearrange("a p w -> (a p) w")).then_inc(w_loaded[slot], 16)
                each(sp, ph.slabs, one)

            def store(dst, src):
                sp.dma_start(dst, src).then_inc(stored, 16)

            sp.dma_start(vec[:, :], A["vec"]).then_inc(sem("vec_in"), 16)
            for k in range(KD):
                sp.dma_start(x[:, k * T:(k + 1) * T], A["x"][:, k * T:(k + 1) * T]).then_inc(sem(f"x_in{k}"), 16)
            sp.dma_start(w_dt[:, :], A["w_dt"]).then_inc(sem("wdt_in"), 16)
            weights("v")
            for dst, name in ((ones, "ones"), (ident, "ident"), (tri, "tri"), (neg, "neg"), (head_rows, "head_rows"),
                              (conv_state, "conv_state"), (ffn_state, "ffn_state")):
                load(dst[:, :], A[name])
            weights("u")
            for name in ("xbc", "outa", "z", "outb", "gu00"):
                weights(name)
            sp.wait_ge(sem("conv_tailed"), XBC)
            store(O["conv_tail"], conv_tail[:, :])
            sp.wait_ge(sem("s_new"), 4 * (NC + 1))
            store(O["ssm_prompt"], s_prompt)
            store(O["ssm_sample"], s_sample)
            for name in ("down00", "gu01"):
                weights(name)
            for layer in range(2):
                if layer:
                    weights("heads_a")
                    weights("ret_a")
                    weights("heads_b")
                    weights("ret_b")
                    weights("gu10")
                    weights("down10")
                    weights("gu11")
                weights(f"down{layer}1")
                weights(f"gu{layer}2")
                weights(f"down{layer}2")
                weights(f"pp{layer}")
                weights(f"gate{layer}")
            sp.wait_ge(sem("f_tailed"), 2 * FT)
            store(O["ffn_tail"], ffn_tail[:, :])
            for k in range(KD):
                sp.wait_ge(sem("y_out"), k + 1)
                store(O["y"][:, k * T:(k + 1) * T], p_proj[:, k * T:(k + 1) * T])
            sp.wait_ge(stored, 16 * (4 + KD))
            sp.wait_ge(sem("gm_v_out"), 16)

        @block.gpsimd
        def _(pool):
            sub, mul = ALU.subtract, ALU.mult

            def phase(name, job=None, per=4):
                def one(n):
                    low_ahead(pool, PH[name], n)
                    if job:
                        job(n)
                each_ahead(pool, PH[name], one, per)

            pool.wait_ge(sem("wdt_hi"), 1)
            nc.gpsimd.tensor_tensor(w_dt_lo[:, :], w_dt[:, :], w_dt_hi[:, :], sub).then_inc(sem("wdt_lo"), 1)
            pool_squares(pool, "n_in", None)
            for k in range(KD):
                if k in (0, 2):
                    split_low(pool, At(k // 2))
                pool_square(pool, "n_in", At(k))
            split_low(pool, At(2))
            split_low(pool, At(3))
            phase("v")
            phase("u")
            pool.wait_ge(sem("gm_in"), 48)
            for c in range(NC + 1):
                rows = CH if c < NC else TS
                pool.wait_ge(sem("gm_scaled"), c + 1)
                v = v_tok[0:rows, c * D:(c + 1) * D]
                nc.gpsimd.tensor_tensor(v, v, gain_rows[0:rows, :], mul).then_inc(sem("gm_vn"), 1)
            phase("xbc")

            def chunk(p, rows):
                pool.wait_ge(sem("x_copied"), 3 * p + 3)
                if p:
                    pool.wait_ge(sem("y_turned"), 2 * p)
                c = NC if p == 0 else p - 1
                three = lambda b, n: b[0:rows, 0:n * SP_].rearrange("p (h q) -> p h q", h=n)
                nc.gpsimd.tensor_tensor(three(y_tok, SH), three(x_tok, SH),
                                        head_rows[0:rows, 2 * SH:3 * SH].unsqueeze(2).broadcast_to([rows, SH, SP_]),
                                        mul).then_inc(sem("y_skip"), 1)
                pool.wait_ge(sem("xs_done"), p + 1)
                if p:
                    pool.wait_ge(sem("st_mm"), 2 * p)
                nc.gpsimd.tensor_tensor(three(xsd, SH), three(xs, SH),
                                        dte[0:rows, c * SH:(c + 1) * SH].unsqueeze(2).broadcast_to([rows, SH, SP_]),
                                        mul).then_inc(sem("xsd_done"), 1)

            chunk(0, TS)
            for p in range(1, NC + 1):
                chunk(p, CH)
                low_ahead(pool, PH["outa"], At(2 * p - 2))
                low_ahead(pool, PH["outa"], At(2 * p - 1))
            phase("z")
            pool_squares(pool, "n_yb", "n_in")
            for n in range(KD):
                pool_square(pool, "n_yb", At(n))
            pool_squares(pool, "n_ffn0", "n_yb")
            phase("outb", lambda n: pool_square(pool, "n_ffn0", n))

            for layer in range(2):
                if layer:
                    def head(name, h, h0):
                        for r_ in range(6):
                            n = (h + -h0) * 6 + r_
                            low_ahead(pool, PH[name], n)
                            if r_ < 2:
                                pool.wait_ge(sem("r_swap"), (h * 2 + (r_ + 1)).v)
                                nc.gpsimd.tensor_tensor(rot_sw, rot_sw, (sin_k, sin_q)[r_], mul)\
                                    .then_inc(sem("r_sin"), 1)
                    heads(pool, head, lambda: phase("ret_a"))
                    pool_squares(pool, "n_ffn1", "n_mix1")
                    phase("ret_b", lambda n: pool_square(pool, "n_ffn1", n))
                off = 0
                for part_, nt in enumerate(FFN_PARTS):
                    gu = PH[f"gu{layer}{part_}"]

                    def gated(n, off=off, gu=gu):
                        if n.mod(2):
                            return
                        t = n.div(2) + (off + layer * FT)
                        q = n.div(2).mod(2)
                        pool.wait_ge(sem("f_silu"), (t + 1).v)
                        pool.wait_ge(tile_read, (n + (gu.g0 - 2)).v)
                        nc.gpsimd.tensor_tensor(fsgr[:, q * T:(q + 1) * T], fsg[:, q * T:(q + 1) * T], rstd[:, :],
                                                mul).then_inc(sem("f_scaled"), 1)
                    phase(f"gu{layer}{part_}", gated)
                    if part_ == 2:
                        pool_squares(pool, PLE[layer], LAYER[layer])
                        phase(f"down{layer}2", lambda n: pool_square(pool, PLE[layer], n))
                    else:
                        phase(f"down{layer}{part_}")
                    off += nt
                phase(f"pp{layer}")
                nxt = ("n_mix1", "n_out")[layer]
                pool_squares(pool, nxt, PLE[layer])
                phase(f"gate{layer}", lambda n: pool_square(pool, nxt, n))

        @block.scalar
        def _(act):
            def run(dst, src, f, signal=None, **kw):
                ins = nc.scalar.activation(dst, src, f, **kw)
                if signal:
                    ins.then_inc(sem(signal), 1)
                return ins

            def phase(name, job=None, per=4, peel=0):
                def one(n):
                    split_ahead(act, PH[name], n)
                    if job:
                        job(n)
                each_ahead(act, PH[name], one, per, peel)

            def updated(name, g0):
                def job(n):
                    act.wait_ge(tile_read, (n + (g0 + 1)).v)
                    act_operand(act, name, n, part(x, n, 0, T))
                return job

            act.wait_ge(sem("vec_in"), 16)
            split_high(act, At(0))
            for k in range(KD):
                act.wait_ge(sem(f"x_in{k}"), 16)
                act_operand(act, "n_in", At(k), part(x, k, 0, T))
                if k == 1:
                    act.wait_ge(sem("wdt_in"), 16)
                    run(w_dt_hi[:, :], w_dt[:, :], ACT.Copy, "wdt_hi")
                    split_high(act, At(1))
            split_high(act, At(2))
            split_high(act, At(3))
            act.wait_ge(sem("eps_set"), 1)
            act_root(act, "n_in")
            phase("v")

            def u_job(n):
                q = n.mod(2)
                if n.k or n.c >= 2:
                    act.wait_ge(sem("v_turned"), (n + -1).v)
                run(v_gelu[:, q * T:(q + 1) * T], part(v_raw, n, 0, T), ACT.Gelu_apprx_tanh, "v_gelu")

            def u_rest(n):
                q = n.mod(2)
                act.wait_ge(sem("v_turned"), (n + 1).v)
                tok = v_tok.rearrange("p (c e) -> p c e", c=NC + 1)
                e = ds((n * P).v, P) if n.k else slice(n.c * P, n.c * P + P)
                run(tok[:, 0:NC, e], four(Q[:, 2 * q, :]), ACT.Copy)
                run(tok[0:TS, NC, e], Q[0:TS, 2 * q + 1, 0:P], ACT.Copy, "v_copied")
                act.wait_ge(tile_read, (n + (PH["u"].g0 + 1)).v)
                run(part(u_g, n, 0, T), part(u_g, n, 0, T), ACT.Gelu_apprx_tanh, "u_gelu")

            act.wait_ge(tile_read, PH["v"].g0 + KD)
            def u_all(n):
                u_job(n)
                split_ahead(act, PH["u"], n)
                u_rest(n)
            each(act, KD, u_all)
            act.wait_ge(sem("v_gelu"), KD)
            for dst, name in ((gain_rows, "gain_rows"), (w_spatial, "w_spatial"), (bs_row[0:1, :], "bs_row")):
                act.dma_start(dst, A[name]).then_inc(sem("gm_in"), 16)
            act.wait_ge(sem("v_copied"), KD)
            for c in range(NC + 1):
                rows = CH if c < NC else TS
                if c >= 2:
                    act.wait_ge(sem("gm_sum"), c - 1)
                run(v_sq[c % 2][0:rows, :], v_tok[0:rows, c * D:(c + 1) * D], ACT.Square, "gm_sq")
            act.wait_ge(sem("gm_sum"), NC + 1)
            n_ = NC * GROUPS
            run(ms_v[:, 0:n_], ms_v[:, 0:n_], ACT.Sqrt, bias=eps[:, 0:1], scale=1.0 / P)
            run(ms_v[0:TS, n_:], ms_v[0:TS, n_:], ACT.Sqrt, "gm_root", bias=eps[0:TS, 0:1], scale=1.0 / P)
            split_ahead(act, PH["xbc"], At(0))
            split_ahead(act, PH["xbc"], At(1))
            act.wait_ge(sem("gm_vn"), NC + 1)
            act.dma_start(O["gm_v"], v_tok[0:TS, NC * D:(NC + 1) * D]).then_inc(sem("gm_v_out"), 16)
            for g in range(GROUPS):
                act.wait_ge(sem("gm_ya"), 2 * g + 2)
                run(part(op_hi[1], g, 0, T), ya[:, (g % 2) * T:(g % 2 + 1) * T], ACT.Copy, "gm_hi")
            act.dma_start(s_sample, A["ssm_state"]).then_inc(sem("s_in_loaded"), 16)

            def conv_out(n):
                q = n.mod(2)
                act.wait_ge(sem("x_steps"), (n * 6 + 6).v)
                tail = xpad[:, q * (T + 6) + TP - TS:(q + 1) * (T + 6)].rearrange("p (a b) -> p a b", a=2)
                run(part(conv_tail, n, 0, 6, 6).rearrange("p (a b) -> p a b", a=2), tail[:, :, TS:TS + 3], ACT.Copy,
                    "conv_tailed")
                at = q * (T + 3)
                run(part(xbc, n, 0, TP), conv[:, at:at + TP], ACT.Silu)
                run(part(xbc, n, TP, TS), conv[:, at + TP + 3:at + T + 3], ACT.Silu, "x_silu")

            def xbc_body(n):
                if n.k or n.c >= 2:
                    split_ahead(act, PH["xbc"], n)
                conv_out(n)
            each(act, XBC, xbc_body, peel=4, least=2)
            act.wait_ge(consts_in, 16 * N_CONSTS)
            run(a_row[:, :], head_rows[:, SH:2 * SH], ACT.Exp)
            act.wait_ge(sem("dt_bias"), 1)
            run(p_a, dt_b, ACT.Abs, "dt_abs")
            act.wait_ge(sem("dt_abs"), 1)
            run(p_b, p_a, ACT.Exp, "dt_exp", scale=-1.0)
            act.wait_ge(sem("cs_copied"), 1)
            run(ecs, cs, ACT.Exp)
            run(dte, dte, ACT.Exp)
            run(etot, etot, ACT.Exp, "decays")

            def chunk(p, rows, slabs):
                c = NC if p == 0 else p - 1
                act.wait_ge(sem("x_turned"), 3 * p + 1)
                if p:
                    act.wait_ge(sem("y_skip"), p)
                    act.wait_ge(sem("xs_done"), p)
                run(x_tok[0:rows, 0:512], Q[0:rows, 0, :], ACT.Copy, "x_copied")
                act.wait_ge(sem("x_turned"), 3 * p + 2)
                run(x_tok[0:rows, 512:D], Q[0:rows, 1, :], ACT.Copy, "x_copied")
                act.wait_ge(sem("x_turned"), 3 * p + 3)
                q2 = Q[0:rows, 2, :]
                if rows == CH:
                    run(bc_tok[0:rows, :], q2, ACT.Copy, "x_copied")
                else:
                    run(bc_tok[0:rows, 0:256], q2[:, 0:256], ACT.Copy)
                    run(two(bc_tok[0:rows, 256:512])[:, :, 0:rows], two(q2[:, 256:512])[:, :, 0:rows], ACT.Copy,
                        "x_copied")
                for b in range(4):
                    act.wait_ge(sem("seg_done"), 16 * p + 4 * b + 4)
                    m = four(mix[0:rows, (b % 2) * 512:(b % 2 + 1) * 512])[:, :, 0:rows]
                    run(m, m, ACT.Exp, "decayed")
                    if slabs and b % 2:
                        split_ahead(act, PH["outa"], At(2 * p - 2 + b // 2))
                for half in range(2):
                    act.wait_ge(sem("y_turned"), 2 * p + half + 1)
                    dst = xbc[:, 4 * half * T:4 * (half + 1) * T].rearrange("p (f t) -> p f t", f=4)
                    src = four(Q[:, half, :])
                    run(dst[:, :, c * CH:c * CH + rows], src[:, :, 0:rows], ACT.Copy, "y_stored")

            chunk(0, TS, False)
            for p in range(1, NC + 1):
                chunk(p, CH, True)

            def z_job(n):
                q = n.mod(2)
                act.wait_ge(tile_read, (n + (PH["z"].g0 + 1)).v)
                zb = z_buf[:, q * T:(q + 1) * T]
                run(zb, zb, ACT.Silu, "z_silu")
            phase("z", z_job)
            for n in range(KD):
                act.wait_ge(sem("yb_made"), n + 1)
                act_operand(act, "n_yb", At(n), part(xbc, n, 0, T))
            act_root(act, "n_yb")

            def outb_job(n):
                act.wait_ge(sem("outb_added"), (n + 1).v)
                act_operand(act, "n_ffn0", n, part(x, n, 0, T))
            phase("outb", outb_job)
            act_root(act, "n_ffn0")

            for layer in range(2):
                if layer:
                    def turn1(h):
                        hh = h + 0
                        act.wait_ge(sem("r_kturn"), (h + 1).v)
                        act.dma_start(s_in, A["ret_state"][ds(h.v, 1), :, :].rearrange("a p e -> (a p) e") if h.k else
                                      A["ret_state"][h.c, :, :]).then_inc(sem("s_in_ret"), 16)
                        run(k_tok[:, 0:NC * RDK], Q[:, 2, :], ACT.Copy, "r_ktok", scale=col("kdec", hh))

                    def turn2(h):
                        act.wait_ge(sem("r_vturn"), (h + 1).v)
                        tok = rv_tok.rearrange("p (c e) -> p c e", c=NC + 1)
                        run(tok[:, 0:NC, 0:P], four(Q[:, 0, :]), ACT.Copy)
                        run(tok[:, 0:NC, P:RDV], four(Q[:, 3, :]), ACT.Copy, "r_vtok")

                    def turn4(h):
                        act.wait_ge(sem("r_state"), (h * 5 + 5).v)
                        for name, src in (("ret_prompt", s_hist[:, (NC - 1) * RDV:]), ("ret_sample", s_out)):
                            dst = O[name][ds(h.v, 1), :, :].rearrange("a p e -> (a p) e") if h.k else O[name][h.c, :, :]
                            act.dma_start(dst, src).then_inc(sem("ret_stored"), 16)
                        act.wait_ge(sem("r_norm"), (h * 16 + 10).v)
                        var = mv.rearrange("p (c two) -> p c two", two=2)
                        run(sd.unsqueeze(2), var[:, :, 1:2], ACT.Sqrt, "r_root", bias=eps[:, 0:1])

                    def turn5(h, tile):
                        for e in range(2):
                            act.wait_ge(sem("r_mix"), (h * 4 + (2 * e + 3)).v)
                            run(part(op_hi[1], tile + e, 0, T), sq[:, e * T:(e + 1) * T],
                                ACT.Copy, "r_mhi")

                    def head(name, h, h0):
                        n = (h + -h0) * 6
                        g0 = n + PH[name].g0
                        prev = h + -1
                        first = not h.k and h.c == 0
                        tile = (prev + (0 if name == "heads_a" and (h.k or h.c < 5) else -4)) * 2
                        for r_ in range(6):
                            if not first:
                                if r_ == 0:
                                    turn1(prev)
                                elif r_ == 1:
                                    turn2(prev)
                                elif r_ == 3:
                                    turn4(prev)
                                elif r_ == 4:
                                    turn5(prev, tile)
                            split_ahead(act, PH[name], n + r_)
                            act_wait = (g0 + (r_ + 1)).v
                            if r_ < 2:
                                act.wait_ge(tile_read, act_wait)
                                if not (first and r_ == 0):
                                    act.wait_ge(sem("r_kq"), (h * 2 + r_).v)
                                run(rot_sw[0:64, :], rot[64:128, :], ACT.Copy)
                                run(rot_sw[64:128, :], rot[0:64, :], ACT.Copy, "r_swap")
                            elif r_ >= 4:
                                act.wait_ge(tile_read, act_wait)
                                gt = g_s[:, (r_ - 4) * T:(r_ - 3) * T]
                                run(gt, gt, ACT.Silu, "r_silu")

                    def drain():
                        turn1(At(7))
                        turn2(At(7))
                        turn4(At(7))
                        turn5(At(7), At(6))
                    run(token[:, 1:2], eps[:, :], ACT.Copy, "ret_stored")
                    heads(act, head, lambda: phase("ret_a"), drain)
                    phase("ret_b", updated("n_ffn1", PH["ret_b"].g0))
                    act_root(act, "n_ffn1")

                off = 0
                for part_, nt in enumerate(FFN_PARTS):
                    gu = PH[f"gu{layer}{part_}"]

                    def gate_up(n, off=off, gu=gu):
                        t = n.div(2) + (off + layer * FT)
                        q = n.div(2).mod(2)
                        if n.mod(2) == 0:
                            act.wait_ge(sem("f_steps"), (t * 5 + 5).v)
                            tail = gpad[:, q * (T + 4) + TP - TS:(q + 1) * (T + 4)]\
                                .rearrange("p (a b) -> p a b", a=2)
                            dst = part(ffn_tail, t, 0, 4, 4).rearrange("p (a b) -> p a b", a=2)
                            run(dst, tail[:, :, TS:TS + 2], ACT.Copy, "f_tailed")
                            at = q * (T + 2)
                            if t.k or t.c >= 2:
                                act.wait_ge(sem("f_scaled"), (t + -1).v)
                            run(fsg[:, q * T:q * T + TP], facc[:, at:at + TP], ACT.Silu)
                            run(fsg[:, q * T + TP:(q + 1) * T], facc[:, at + TP + 2:at + T + 2], ACT.Silu,
                                "f_silu")
                        else:
                            act.wait_ge(tile_read, (n + (gu.g0 + 1)).v)
                            run(part(op_hi[HID[layer]], n.div(2), 0, T), hid[:, q * T:(q + 1) * T], ACT.Copy,
                                "f_hi")
                    phase(gu.name, gate_up, peel=0 if off or layer else 4)
                    if layer == 0 and part_ == 0:
                        act.wait_ge(stored, 16 * 3)
                        for dst, t_ in ((cos_q, "cos_q"), (sin_q, "sin_q"), (cos_k, "cos_k"), (sin_k, "sin_k"),
                                        (dmat, "dmat"), (qdec, "qdec")):
                            act.dma_start(dst, A[t_]).then_inc(sem("tables_in"), 16)
                    if part_ == 1:
                        act.dma_start(p_raw, A["p"][:, layer * 2 * T:(layer + 1) * 2 * T])\
                            .then_inc(sem(f"p_in{layer}"), 16)
                    if part_ == 2:
                        act.wait_ge(sem(f"p_in{layer}"), 16)
                        run(op_hi[HID[layer]][:, 6 * T:8 * T], p_raw, ACT.Copy, "p_hi")
                        down = PH[f"down{layer}2"]
                        phase(down.name, updated(PLE[layer], down.g0))
                    else:
                        phase(f"down{layer}{part_}")
                    off += nt
                phase(f"pp{layer}")
                act_root(act, PLE[layer])
                nxt = ("n_mix1", "n_out")[layer]

                def gate_job(n):
                    q = n.mod(2)
                    act.wait_ge(tile_read, (n + (PH[f"gate{layer}"].g0 + 1)).v)
                    gt = gate_t[:, q * T:(q + 1) * T]
                    run(gt, gt, ACT.Sigmoid, "g_sig")
                    act.wait_ge(sem("gate_added"), (n + (1 + layer * KD)).v)
                    if layer == 0:
                        act_operand(act, nxt, n, part(x, n, 0, T))
                    else:
                        act_square(act, nxt, n, part(x, n, 0, T))
                phase(f"gate{layer}", gate_job)
                act_root(act, nxt)
            act.wait_ge(sem("ret_stored"), 1 + 32 * RH)

        @block.tensor
        def _(pe):
            def mm(out, w, o, start=True, stop=True):
                return nc.tensor.matmul(out, w, o, start=start, stop=stop)

            def phase(name, ops, ready=None, per=4, hook=None, k0=0, start=0):
                ph = PH[name]

                def one(n):
                    slab(pe, ph, n, ops, ready, k0)
                    if hook and not n.k and n.c == 0:
                        hook()
                each(pe, ph.slabs, one, per, peel=4 if hook else 0, least=2)

            def norm(name):
                def hook():
                    if name == "n_in":
                        pe.wait_ge(consts_in, 16 * N_CONSTS)
                    mean_square(pe, name)
                return hook

            phase("v", 0, (nsem("lo"), ncount("n_in", "lo", 1)), hook=norm("n_in"))

            def u_body(n):
                slab(pe, PH["u"], n, 0)
                q = n.mod(2)
                pe.wait_ge(sem("v_gelu"), (n + 1).v)
                if n.k or n.c >= 2:
                    pe.wait_ge(sem("v_copied"), (n + -1).v)
                elif n.c == 0:
                    pe.wait_ge(nsem("root"), ncount("n_in", "root", 1))
                v = v_gelu[:, q * T:(q + 1) * T]
                for c in range(NC):
                    nc.tensor.transpose(Q[:, 2 * q, c * CH:(c + 1) * CH], v[:, c * CH:(c + 1) * CH], ident[:, :])
                nc.tensor.transpose(Q[0:TS, 2 * q + 1, 0:P], v[:, TP:T], ident[:, :]).then_inc(sem("v_turned"), 1)
            each(pe, KD, u_body)
            xb = PH["xbc"]
            slab(pe, xb, At(0), 0)
            slab(pe, xb, At(1), 0)
            pe.wait_ge(sem("gm_mask"), 1)
            pe.wait_ge(sem("gm_vn"), NC + 1)
            for g in range(GROUPS):
                if g >= 2:
                    pe.wait_ge(sem("gm_ya"), 2 * g - 2)
                q = 2 * (g % 2)
                e = slice(g * P, (g + 1) * P)
                for c in range(NC + 1):
                    rows = CH if c < NC else TS
                    out = Q[:, q, c * CH:(c + 1) * CH] if c < NC else Q[:, q + 1, 0:TS]
                    mm(out, v_tok[0:rows, c * D + g * P:c * D + (g + 1) * P], w_spatial[0:rows, g * P:g * P + rows],
                       stop=False)
                    last = mm(out, ones[0:1, :], bs_row[0:1, g * P:g * P + rows], start=False)
                last.then_inc(sem("gm_s"), 1)

            def rest(n):
                slab(pe, xb, n + 2, 0)
            each(pe, XBC - 2, rest, least=2)
            pe.wait_ge(tile_read, DT_GROUP - 1)
            pe.wait_ge(sem("wdt_lo"), 1)
            qd_ = DT_GROUP % 2
            for k in range(KD):
                for j, (w, o) in enumerate(((w_dt_hi, op_hi[0]), (w_dt_hi, op_lo[0]), (w_dt_lo, op_hi[0]))):
                    for half in range(2):
                        size = HALF + TS * half
                        at = k * T + half * HALF
                        last = mm(proj[0:SH, 2 * qd_ + half, 0:size], w[:, k * SH:(k + 1) * SH], o[:, at:at + size],
                                  start=(k == 0 and j == 0), stop=(k == KD - 1 and j == 2))
            last.then_inc(tile_done, 1)
            pe.wait_ge(tile_read, DT_GROUP + 1)
            pe.wait_ge(sem("gm_ya"), 2 * GROUPS)
            for c in range(NC + 1):
                rows = CH if c < NC else TS
                last = nc.tensor.transpose(Q[0:rows, 0, c * SH:(c + 1) * SH], dt_t[0:SH, c * CH:c * CH + rows],
                                           ident[0:SH, 0:SH])
            last.then_inc(sem("dt_turned"), 1)
            pe.wait_ge(sem("da_done"), 1)
            mm(Q[:, 1, 0:NP_], tri[:, :], da)
            mm(Q[:, 1, 128:128 + NC * SH], ones[:, :], da[:, 0:NC * SH])
            mm(Q[:, 1, 128 + NC * SH:128 + NP_], ones[0:TS, :], da[0:TS, NC * SH:NP_]).then_inc(sem("cs_mm"), 1)

            def chunk(p, rows, slabs):
                c = NC if p == 0 else p - 1
                cols = lambda f: xbc[:, f * T + c * CH:f * T + c * CH + rows]
                state = s_sample if p == 0 else s_prompt
                hc = c * SH
                if p == 0:
                    pe.wait_ge(sem("x_silu"), XBC)
                    pe.wait_ge(sem("cs_copied"), 1)
                else:
                    pe.wait_ge(sem("y_stored"), 2 * p)
                for half in range(2):
                    for f in range(4):
                        last = nc.tensor.transpose(Q[0:rows, half, f * P:(f + 1) * P], cols(4 * half + f), ident[:, :])
                    last.then_inc(sem("x_turned"), 1)
                if p:
                    pe.wait_ge(sem("s_new"), 4 * p)
                for g in range(2):
                    nc.tensor.transpose(Q[0:rows, 2, g * P:(g + 1) * P], cols(8 + g), ident[:, :])
                for g in range(2):
                    last = mm(Q[0:rows, 2, 256 + g * P:256 + g * P + rows], cols(8 + g), cols(10 + g))
                last.then_inc(sem("x_turned"), 1)

                def rows_of_cs(b):
                    if b == 1:
                        pe.wait_ge(sem("x_copied"), 3 * p + 3)
                    elif b >= 2:
                        pe.wait_ge(sem("seg_done"), 16 * p + 4 * (b - 1))
                    bank = 3 - b % 2
                    for j in range(4):
                        h = hc + 4 * b + j
                        last = mm(Q[0:rows, bank, j * P:j * P + rows], da[0:rows, h:h + 1].broadcast_to([rows, rows]),
                                  tri[0:rows, 0:rows])
                    last.then_inc(sem("cs_rows"), 1)

                def diagonal(b):
                    pe.wait_ge(sem("mixed"), 4 * p + b + 1)
                    if b == 0:
                        pe.wait_ge(sem("x_copied"), 3 * p + 2)
                    for j in range(4):
                        h = 4 * b + j
                        m = mix[0:rows, (b % 2) * 512 + j * P:(b % 2) * 512 + j * P + rows]
                        last = mm(Q[0:rows, b // 2, (h % 8) * SP_:(h % 8 + 1) * SP_], m,
                                  xs[0:rows, h * SP_:(h + 1) * SP_])
                    last.then_inc(sem("y_mm"), 1)

                for b in range(4):
                    rows_of_cs(b)
                if slabs:
                    slab(pe, PH["outa"], At(2 * p - 2), 1, (sem("gm_lo"), 1))
                diagonal(0)
                diagonal(1)
                if slabs:
                    slab(pe, PH["outa"], At(2 * p - 1), 1)
                diagonal(2)
                diagonal(3)
                pe.wait_ge(sem("seg_done"), 16 * p + 16)
                pe.wait_ge(sem("s_zero"), 1)
                pe.wait_ge(sem("s_in_loaded"), 16)
                for g in range(2):
                    mm(Q[0:rows, 2 + g, :], cols(10 + g), state[:, g * 512:(g + 1) * 512]).then_inc(sem("y_off"), 1)
                pe.wait_ge(sem("xsd_done"), p + 1)
                for g in range(2):
                    pe.wait_ge(sem("y_scaled"), 2 * p + g + 1)
                    mm(Q[:, 2 + g, :], bc_tok[0:rows, g * P:(g + 1) * P], xsd[0:rows, g * 512:(g + 1) * 512])\
                        .then_inc(sem("st_mm"), 1)
                pe.wait_ge(sem("y_full"), 2 * p + 2)
                for half in range(2):
                    for f in range(4):
                        last = nc.tensor.transpose(Q[:, half, f * P:f * P + rows],
                                                   y_tok[0:rows, (4 * half + f) * P:(4 * half + f + 1) * P],
                                                   ident[0:rows, 0:rows])
                    last.then_inc(sem("y_turned"), 1)

            chunk(0, TS, False)
            for p in range(1, NC + 1):
                chunk(p, CH, True)
            phase("z", 0)
            phase("outb", 0, (nsem("lo"), ncount("n_yb", "lo", 1)), hook=norm("n_yb"))

            for layer in range(2):
                if layer:
                    def turn1(h):
                        pe.wait_ge(sem("r_kq"), (h * 2 + 2).v)
                        pe.wait_ge(sem("r_mix"), (h * 4 + 1).v)
                        for c in range(NC):
                            t = slice(c * CH, (c + 1) * CH)
                            last = mm(Q[:, 0, t], k_t[:, t], q_t[:, t])
                        last.then_inc(sem("r_scores"), 1)
                        mm(Q[0:TS, 1, 0:TS], k_t[:, TP:T], q_t[:, TP:T])
                        nc.tensor.transpose(Q[0:TS, 1, P:2 * P], k_t[:, TP:T], ident[:, :])
                        for c in range(NC):
                            t = slice(c * CH, (c + 1) * CH)
                            last = nc.tensor.transpose(Q[:, 2, t], k_t[:, t], ident[:, :])
                        last.then_inc(sem("r_kturn"), 1)

                    def turn2(h):
                        pe.wait_ge(sem("r_scd"), (h * 5 + 5).v)
                        for c in range(NC):
                            t = slice(c * CH, (c + 1) * CH)
                            nc.tensor.transpose(Q[:, 0, t], v_t[:, t], ident[:, :])
                            nc.tensor.transpose(Q[:, 3, t], v_t[:, T + c * CH:T + (c + 1) * CH], ident[:, :])
                        for e in range(2):
                            last = nc.tensor.transpose(Q[0:TS, 1, e * P:(e + 1) * P], v_t[:, e * T + TP:(e + 1) * T],
                                                       ident[:, :])
                        last.then_inc(sem("r_vturn"), 1)

                    def turn3(h):
                        pe.wait_ge(sem("r_ktok"), (h + 1).v)
                        pe.wait_ge(sem("r_vtok"), (h + 1).v)
                        pe.wait_ge(sem("r_vs"), (h + 1).v)
                        for c in range(NC):
                            mm(Q[:, 2 + c // 2, (c % 2) * RDV:(c % 2 + 1) * RDV], k_tok[:, c * RDK:(c + 1) * RDK],
                               rv_tok[:, c * RDV:(c + 1) * RDV])
                        mm(Q[:, 1, 0:RDV], k_tok[0:TS, NC * RDK:], rv_tok[0:TS, NC * RDV:]).then_inc(sem("r_kv"), 1)

                    def turn4(h):
                        pe.wait_ge(sem("r_state"), (h * 5 + 5).v)
                        for c in range(NC):
                            out = Q[:, 2 * (c // 2), (c % 2) * RDV:(c % 2 + 1) * RDV]
                            mm(out, sc[:, c * CH:(c + 1) * CH], rv_tok[:, c * RDV:(c + 1) * RDV], stop=(c == 0))
                            if c:
                                mm(out, qd[:, c * CH:(c + 1) * CH], s_hist[:, (c - 1) * RDV:c * RDV], start=False)
                        out = Q[0:TS, 1, 0:RDV]
                        mm(out, sc[0:TS, TP:T], rv_tok[0:TS, NC * RDV:], stop=False)
                        mm(out, qd[:, TP:T], s_in, start=False).then_inc(sem("r_y"), 1)

                    def turn5(h):
                        pe.wait_ge(sem("r_norm"), (h * 16 + 16).v)
                        for e, bank in ((0, 3), (1, 0)):
                            for c in range(NC):
                                at = c * RDV + e * P
                                nc.tensor.transpose(Q[:, bank, c * CH:(c + 1) * CH], yn[:, at:at + P], ident[:, :])
                        for e in range(2):
                            at = NC * RDV + e * P
                            last = nc.tensor.transpose(Q[:, 1, e * TS:(e + 1) * TS], yn[0:TS, at:at + P],
                                                       ident[0:TS, 0:TS])
                        last.then_inc(sem("r_yturn"), 1)

                    turns = (turn1, turn2, turn3, turn4, turn5)

                    def head(name, h, h0):
                        n = (h + -h0) * 6
                        first = not h.k and h.c == 0
                        for r_ in range(6):
                            if not first and r_ < 5:
                                turns[r_](h + -1)
                            slab(pe, PH[name], n + r_, 0, (nsem("lo"), ncount("n_mix1", "lo", 1)) if first and r_ == 0 else None)
                            if first and r_ == 0:
                                mean_square(pe, "n_mix1")

                    def drain():
                        for turn in turns:
                            turn(At(7))
                    heads(pe, head, lambda: phase("ret_a", 1, (sem("r_mlo"), 1)), drain)
                    phase("ret_b", 1, (sem("r_mlo"), 9))
                off = 0
                for part_, nt in enumerate(FFN_PARTS):
                    if part_ == 0:
                        phase(f"gu{layer}0", 1 - HID[layer], (nsem("lo"), ncount(LAYER[layer], "lo", 1)), hook=norm(LAYER[layer]))
                    else:
                        phase(f"gu{layer}{part_}", 1 - HID[layer])
                    phase(f"down{layer}{part_}", HID[layer], (sem("f_lo"), layer * FT + off + 1))
                    off += nt
                pe.wait_ge(sem("p_lo"), layer + 1)
                phase(f"pp{layer}", HID[layer], k0=6)
                mean_square(pe, PLE[layer])
                phase(f"gate{layer}", 1 - HID[layer], (nsem("lo"), ncount(PLE[layer], "lo", 1)))
            mean_square(pe, "n_out")

        def retention_dve(dve, scaled, add_to_x, group):
            add, sub, mul = ALU.add, ALU.subtract, ALU.mult
            tt = nc.vector.tensor_tensor
            stt = nc.vector.scalar_tensor_tensor
            dve_rstd(dve, "n_mix1")
            nc.vector.memset(mv, 1.0)
            nc.vector.memset(token[:, 0:1], 0.0).then_inc(sem("r_mix"), 1)
            dve.wait_ge(sem("tables_in"), 16 * 6)

            def table(b, h):
                return b[:, ds((h * CH).v, CH)] if h.k else b[:, h.c * CH:(h.c + 1) * CH]

            def turn1(h):
                over = lambda b: b.unsqueeze(1).broadcast_to([P, NC, CH])
                dve.wait_ge(sem("r_scores"), (h + 1).v)
                tt(four(sc[:, 0:TP]), four(Q[:, 0, :]), over(table(dmat, h)), mul).then_inc(sem("r_scd"), 1)
                tt(four(qd[:, 0:TP]), four(q_t[:, 0:TP]), over(table(qdec, h)), mul).then_inc(sem("r_scd"), 1)
                tt(qd[:, TP:T], q_t[:, TP:T], table(qdec, h)[:, 0:TS], mul).then_inc(sem("r_scd"), 1)
                dve.wait_ge(sem("r_kturn"), (h + 1).v)
                tt(sc[0:TS, TP:T], Q[0:TS, 1, 0:TS], table(dmat, h)[0:TS, 0:TS], mul).then_inc(sem("r_scd"), 1)
                nc.vector.tensor_scalar(k_tok[0:TS, NC * RDK:], Q[0:TS, 1, P:2 * P], col("kdec_s", h)[0:TS, :], None,
                                        mul).then_inc(sem("r_scd"), 1)

            def turn2(h):
                dve.wait_ge(sem("r_vturn"), (h + 1).v)
                nc.vector.tensor_copy(rv_tok[0:TS, NC * RDV:], Q[0:TS, 1, 0:RDV]).then_inc(sem("r_vs"), 1)

            def turn3(h):
                dve.wait_ge(sem("r_kv"), (h + 1).v)
                dve.wait_ge(sem("ret_stored"), (h * 32 + 1).v)
                nc.vector.tensor_copy(s_hist[:, 0:RDV], Q[:, 2, 0:RDV]).then_inc(sem("r_state"), 1)
                for c in range(1, NC):
                    dve.wait_ge(sem("r_state"), (h * 5 + c).v)
                    stt(out=s_hist[:, c * RDV:(c + 1) * RDV], in0=s_hist[:, (c - 1) * RDV:c * RDV],
                        scalar=col("g_chunk", h), in1=Q[:, 2 + c // 2, (c % 2) * RDV:(c % 2 + 1) * RDV],
                        op0=mul, op1=add).then_inc(sem("r_state"), 1)
                dve.wait_ge(sem("s_in_ret"), (h * 16 + 16).v)
                stt(out=s_out, in0=s_in, scalar=col("g_sample", h), in1=Q[:, 1, 0:RDV], op0=mul, op1=add)\
                    .then_inc(sem("r_state"), 1)

            def turn4(h):
                dve.wait_ge(sem("r_y"), (h + 1).v)

                def y(c):
                    if c == NC:
                        return Q[0:TS, 1, 0:RDV]
                    return Q[:, 2 * (c // 2), (c % 2) * RDV:(c % 2 + 1) * RDV]
                for c in range(NC + 1):
                    rows = CH if c < NC else TS
                    nc.vector.bn_stats(stats[0:rows, c * 6:(c + 1) * 6], y(c)).then_inc(sem("r_norm"), 1)
                dve.wait_ge(sem("r_norm"), (h * 16 + 5).v)
                nc.vector.memset(token[:, 0:1], 0.0)
                for c in range(NC + 1):
                    rows = CH if c < NC else TS
                    nc.vector.bn_aggr(mv[0:rows, c * 2:(c + 1) * 2], stats[0:rows, c * 6:(c + 1) * 6])\
                        .then_inc(sem("r_norm"), 1)
                dve.wait_ge(sem("r_root"), (h + 1).v)
                nc.vector.reciprocal(sd, sd).then_inc(sem("r_norm"), 1)
                dve.wait_ge(sem("r_norm"), (h * 16 + 11).v)
                for c in range(NC + 1):
                    rows = CH if c < NC else TS
                    nc.vector.tensor_scalar(yn[0:rows, c * RDV:(c + 1) * RDV], y(c), mv[0:rows, 2 * c:2 * c + 1],
                                            sd[0:rows, c:c + 1], sub, mul).then_inc(sem("r_norm"), 1)

            def turn5(h, tile):
                dve.wait_ge(sem("r_yturn"), (h + 1).v)
                dve.wait_ge(sem("r_silu"), (h * 2 + 2).v)
                for e, bank in ((0, 3), (1, 0)):
                    gain = col("ret_norm", h * 2 + e)
                    stt(out=sq[:, e * T:e * T + TP], in0=Q[:, bank, :], scalar=gain, in1=g_s[:, e * T:e * T + TP],
                        op0=mul, op1=mul).then_inc(sem("r_mix"), 1)
                    stt(out=sq[:, e * T + TP:(e + 1) * T], in0=Q[:, 1, e * TS:(e + 1) * TS], scalar=gain,
                        in1=g_s[:, e * T + TP:(e + 1) * T], op0=mul, op1=mul).then_inc(sem("r_mix"), 1)
                for e in range(2):
                    dve.wait_ge(sem("r_mhi"), (h * 2 + (e + 1)).v)
                    tt(part(op_lo[1], tile + e, 0, T), sq[:, e * T:(e + 1) * T], part(op_hi[1], tile + e, 0, T), sub)\
                        .then_inc(sem("r_mlo"), 1)

            def rope(h, r_, g):
                m = h * 2 + r_
                dst, cos = ((k_t, cos_k), (q_t, cos_q))[r_]
                scaled(g, lambda c, w: rot[:, c:c + w])
                dve.wait_ge(tile_read, (g + 1).v)
                tt(dst, rot, cos, mul).then_inc(sem("r_rope"), 1)
                dve.wait_ge(sem("r_rope"), (m + 1).v)
                dve.wait_ge(sem("r_sin"), (m + 1).v)
                tt(dst, dst, rot_sw, add).then_inc(sem("r_kq"), 1)

            def head(name, h, h0):
                n = (h + -h0) * 6
                prev = h + -1
                first = not h.k and h.c == 0
                tile = (prev + (0 if h.k or h.c < 5 else -4)) * 2
                for r_ in range(6):
                    if not first and r_ < 5:
                        if r_ == 4:
                            turn5(prev, tile)
                        else:
                            (turn1, turn2, turn3, turn4)[r_](prev)
                    g = group(name, n + r_)
                    if r_ < 2:
                        rope(h, r_, g)
                    else:
                        buf = (v_t, v_t, g_s, g_s)[r_ - 2]
                        at = (r_ % 2) * T
                        scaled(g, lambda c, w: buf[:, at + c:at + c + w])

            def drain():
                for turn in (turn1, turn2, turn3, turn4):
                    turn(At(7))
                turn5(At(7), At(6))
            heads(dve, head, lambda: each(dve, KD, lambda n: add_to_x(group("ret_a", n), n)), drain)

            def last(n):
                add_to_x(group("ret_b", n), n)
                dve_operand(dve, "n_ffn1", n, part(x, n, 0, T))
            each(dve, KD, last)

        @block.vector
        def _(dve):
            add, sub, mul = ALU.add, ALU.subtract, ALU.mult
            tt = nc.vector.tensor_tensor
            stt = nc.vector.scalar_tensor_tensor

            def scaled(g, dst, signal=None, rows=P, factor=None, f_at=0):
                by = rstd if factor is None else factor
                dve.wait_ge(tile_done, (g + 1).v)
                a = tt(two(dst(0, TP)), out_prompt(g, rows), two(by[0:rows, f_at:f_at + TP]), mul)
                if signal:
                    a.then_inc(sem(signal), 1)
                tt(dst(TP, TS), out_sample(g, rows), by[0:rows, f_at + TP:f_at + T], mul).then_inc(tile_read, 1)

            def add_to_x(g, n):
                dve.wait_ge(tile_done, (g + 1).v)
                tt(two(part(x, n, 0, TP)), out_prompt(g), two(part(x, n, 0, TP)), add)
                tt(part(x, n, TP, TS), out_sample(g), part(x, n, TP, TS), add).then_inc(tile_read, 1)

            def group(name, n):
                return n + PH[name].g0

            nc.vector.memset(eps[:, :], EPS).then_inc(sem("eps_set"), 1)
            dve.wait_ge(sem("vec_in"), 16)
            for k in range(KD):
                dve_operand(dve, "n_in", At(k), part(x, k, 0, T))
            dve_rstd(dve, "n_in")

            each(dve, KD, lambda n: scaled(group("v", n), lambda c, w: part(v_raw, n, c, w)))
            each(dve, KD, lambda n: scaled(group("u", n), lambda c, w: part(u_g, n, c, w)))
            dve.wait_ge(sem("gm_in"), 48)
            nc.vector.memset(w_spatial.rearrange("p (g i) -> p g i", g=GROUPS)[64:128, :, 0:64], 0.0)\
                .then_inc(sem("gm_mask"), 1)
            for c in range(NC + 1):
                rows = CH if c < NC else TS
                dve.wait_ge(sem("gm_sq"), c + 1)
                nc.vector.tensor_reduce(ms_v[0:rows, c * GROUPS:(c + 1) * GROUPS],
                                        v_sq[c % 2][0:rows, :].rearrange("p (g e) -> p g e", g=GROUPS), AX.X, add)\
                    .then_inc(sem("gm_sum"), 1)
            dve.wait_ge(sem("gm_root"), 1)
            n_ = NC * GROUPS
            nc.vector.reciprocal(ms_v[:, 0:n_], ms_v[:, 0:n_])
            nc.vector.reciprocal(ms_v[0:TS, n_:], ms_v[0:TS, n_:]).then_inc(sem("gm_rms"), 1)
            dve.wait_ge(sem("gm_rms"), 1)
            for c in range(NC + 1):
                rows = CH if c < NC else TS
                v = v_tok[0:rows, c * D:(c + 1) * D].rearrange("p (g e) -> p g e", g=GROUPS)
                tt(v, v, ms_v[0:rows, c * GROUPS:(c + 1) * GROUPS].unsqueeze(2).broadcast_to([rows, GROUPS, P]), mul)\
                    .then_inc(sem("gm_scaled"), 1)
            dve.wait_ge(sem("u_gelu"), KD)

            def ya_low(g):
                dve.wait_ge(sem("gm_hi"), g + 1)
                tt(part(op_lo[1], g, 0, T), ya[:, (g % 2) * T:(g % 2 + 1) * T], part(op_hi[1], g, 0, T), sub)\
                    .then_inc(sem("gm_lo"), 1)
            for g in range(GROUPS):
                dve.wait_ge(sem("gm_s"), g + 1)
                if g >= 2:
                    dve.wait_ge(sem("gm_lo"), g - 1)
                at = (g % 2) * T
                q = 2 * (g % 2)
                tt(ya[:, at:at + TP], Q[:, q, :], part(u_g, g, 0, TP), mul).then_inc(sem("gm_ya"), 1)
                tt(ya[:, at + TP:at + T], Q[:, q + 1, 0:TS], part(u_g, g, TP, TS), mul).then_inc(sem("gm_ya"), 1)
                if g:
                    ya_low(g - 1)
            ya_low(GROUPS - 1)

            dve.wait_ge(sem("gm_v_out"), 16)
            for q in range(2):
                nc.vector.memset(xpad[:, q * (T + 6):q * (T + 6) + 3], 0.0)

            def conv_body(n):
                q = n.mod(2)
                at = q * (T + 6)
                if n.k or n.c >= 2:
                    dve.wait_ge(sem("x_silu"), (n + -1).v)
                scaled(group("xbc", n), lambda c, w: xpad[:, at + 3 + c + (3 if c else 0):at + 3 + c + (3 if c else 0) + w],
                       "x_steps")
                nc.vector.tensor_copy(xpad[:, at + 3 + TP:at + 6 + TP], part(conv_state, n, 0, 3, 3))\
                    .then_inc(sem("x_steps"), 1)
                acc = conv[:, q * (T + 3):(q + 1) * (T + 3)]
                for tap in range(4):
                    dve.wait_ge(sem("x_steps"), (n * 6 + (2 + tap)).v)
                    src = xpad[:, at + tap:at + tap + T + 3]
                    w = col("ssm_w", n + tap * XBC)
                    if tap == 0:
                        dve.wait_ge(tile_read, (group("xbc", n) + 1).v)
                        nc.vector.tensor_scalar(acc, src, w, col("ssm_b", n), mul, add).then_inc(sem("x_steps"), 1)
                    else:
                        stt(out=acc, in0=src, scalar=w, in1=acc, op0=mul, op1=add).then_inc(sem("x_steps"), 1)
            each(dve, XBC, conv_body, peel=4, least=2)

            g = At(DT_GROUP)
            scaled(g, lambda c, w: dt_t[0:SH, c:c + w], rows=SH)
            steps = [0]

            def link(ins):
                steps[0] += 1
                ins.then_inc(sem("dt_steps"), 1)
                dve.wait_ge(sem("dt_steps"), steps[0])

            link(nc.vector.memset(dt_b, 0.0))
            dve.wait_ge(sem("dt_turned"), 1)
            n_ = NC * SH
            nc.vector.tensor_copy(dt_b[:, 0:n_], Q[:, 0, 0:n_])
            link(nc.vector.tensor_copy(dt_b[0:TS, n_:], Q[0:TS, 0, n_:NP_]))
            by_head = lambda b: b.rearrange("p (c h) -> p c h", h=SH)
            spread = lambda row: row.unsqueeze(1).broadcast_to([P, NC + 1, SH])
            tt(by_head(dt_b), by_head(dt_b), spread(head_rows[:, 0:SH]), add).then_inc(sem("dt_bias"), 1)
            dve.wait_ge(sem("dt_exp"), 1)
            link(nc.vector.tensor_scalar(p_c, p_b, 2.0, None, add))
            link(nc.vector.reciprocal(p_c, p_c))
            link(tt(p_c, p_c, p_b, mul))
            link(tt(p_d, p_c, p_c, mul))
            link(nc.vector.tensor_scalar(p_a, p_d, 1.0 / 17, 1.0 / 15, mul, add))
            for k in (13, 11, 9, 7, 5, 3):
                link(tt(p_a, p_a, p_d, mul))
                link(nc.vector.tensor_scalar(p_a, p_a, 1.0 / k, None, add))
            link(tt(p_a, p_a, p_d, mul))
            link(stt(out=p_a, in0=p_a, scalar=1.0, in1=p_c, op0=add, op1=mul))
            link(nc.vector.tensor_scalar(dt_b, dt_b, 0.0, None, ALU.max))
            link(stt(out=dt_b, in0=p_a, scalar=2.0, in1=dt_b, op0=mul, op1=add))
            link(stt(out=by_head(da), in0=by_head(dt_b), scalar=-1.0, in1=spread(a_row[:, :]), op0=mul, op1=mul))
            nc.vector.memset(da[32:64, n_:], 0.0)
            nc.vector.memset(da[64:128, n_:], 0.0).then_inc(sem("da_done"), 1)
            nc.vector.memset(s_prompt, 0.0).then_inc(sem("s_zero"), 1)
            dve.wait_ge(sem("cs_mm"), 1)
            link(nc.vector.tensor_copy(cs, Q[:, 1, 0:NP_]))
            nc.vector.tensor_copy(etot, Q[:, 1, 128:128 + NP_])
            tt(dte, Q[:, 1, 128:128 + NP_], cs, sub).then_inc(sem("cs_copied"), 1)
            dve.wait_ge(sem("decays"), 1)
            dve.wait_ge(sem("s_in_loaded"), 16)

            def chunk(p, rows, slabs):
                c = NC if p == 0 else p - 1
                state = s_sample if p == 0 else s_prompt
                heads3 = lambda b: b[0:rows, :].rearrange("p (h q) -> p h q", q=SP_)
                per_head = lambda b, h0, nh, rows: b[0:rows, c * SH + h0:c * SH + h0 + nh].unsqueeze(2)\
                    .broadcast_to([rows, nh, SP_])
                dve.wait_ge(sem("x_copied"), 3 * p + 2)
                if p:
                    dve.wait_ge(sem("xsd_done"), p)
                tt(heads3(xs), heads3(x_tok), per_head(dt_b, 0, SH, rows), mul).then_inc(sem("xs_done"), 1)

                def segments(b):
                    dve.wait_ge(sem("cs_rows"), 4 * p + b + 1)
                    if b >= 2:
                        dve.wait_ge(sem("y_mm"), 4 * p + b - 1)
                    elif p:
                        dve.wait_ge(sem("y_mm"), 4 * p - 1 + b)
                    for j in range(4):
                        h = c * SH + 4 * b + j
                        at = (b % 2) * 512 + j * P
                        stt(out=mix[0:rows, at:at + rows], in0=Q[0:rows, 3 - b % 2, j * P:j * P + rows],
                            scalar=cs[0:rows, h:h + 1], in1=neg[0:rows, 0:rows], op0=sub, op1=ALU.min)\
                            .then_inc(sem("seg_done"), 1)

                def mixed(b):
                    dve.wait_ge(sem("decayed"), 4 * p + b + 1)
                    dve.wait_ge(sem("x_copied"), 3 * p + 3)
                    m = four(mix[0:rows, (b % 2) * 512:(b % 2 + 1) * 512])[:, :, 0:rows]
                    cb = bc_tok[0:rows, 256 + (b // 2) * P:256 + (b // 2) * P + rows]
                    tt(m, m, cb.unsqueeze(1).broadcast_to([rows, 4, rows]), mul).then_inc(sem("mixed"), 1)

                segments(0)
                segments(1)
                mixed(0)
                mixed(1)
                if slabs:
                    n = At(2 * p - 2)
                    add_to_x(group("outa", n), n)
                segments(2)
                segments(3)
                mixed(2)
                mixed(3)
                if slabs:
                    n = At(2 * p - 1)
                    add_to_x(group("outa", n), n)
                dve.wait_ge(sem("y_mm"), 4 * p + 4)
                dve.wait_ge(sem("xsd_done"), p + 1)
                dve.wait_ge(sem("y_skip"), p + 1)
                for g in range(2):
                    half = slice(g * 512, (g + 1) * 512)
                    dve.wait_ge(sem("y_off"), 2 * p + g + 1)
                    tt(heads3(xs[:, half]), Q[0:rows, 2 + g, :].rearrange("p (h q) -> p h q", q=SP_),
                       per_head(ecs, 8 * g, 8, rows), mul).then_inc(sem("y_scaled"), 1)
                for g in range(2):
                    half = slice(g * 512, (g + 1) * 512)
                    dve.wait_ge(sem("y_scaled"), 2 * p + g + 1)
                    tt(xs[0:rows, half], Q[0:rows, g, :], xs[0:rows, half], add).then_inc(sem("y_sum"), 1)
                for g in range(2):
                    half = slice(g * 512, (g + 1) * 512)
                    dve.wait_ge(sem("y_sum"), 2 * p + g + 1)
                    tt(y_tok[0:rows, half], y_tok[0:rows, half], xs[0:rows, half], add).then_inc(sem("y_full"), 1)
                for g in range(2):
                    s3 = state[:, g * 512:(g + 1) * 512].rearrange("p (h q) -> p h q", q=SP_)
                    tt(s3, s3, per_head(etot, 8 * g, 8, P), mul).then_inc(sem("s_new"), 1)
                for g in range(2):
                    dve.wait_ge(sem("st_mm"), 2 * p + g + 1)
                    dve.wait_ge(sem("s_new"), 4 * p + g + 1)
                    half = slice(g * 512, (g + 1) * 512)
                    tt(state[:, half], Q[:, 2 + g, :], state[:, half], add).then_inc(sem("s_new"), 1)

            chunk(0, TS, False)
            for p in range(1, NC + 1):
                chunk(p, CH, True)

            dve.wait_ge(sem("y_stored"), 2 * (NC + 1))

            def z_body(n):
                q = n.mod(2)
                zb = z_buf[:, q * T:(q + 1) * T]
                scaled(group("z", n), lambda c, w: zb[:, c:c + w])
                dve.wait_ge(sem("z_silu"), (n + 1).v)
                tt(part(xbc, n, 0, T), part(xbc, n, 0, T), zb, mul).then_inc(sem("yb_made"), 1)
            each(dve, KD, z_body)
            for n in range(KD):
                dve_operand(dve, "n_yb", At(n), part(xbc, n, 0, T))
            dve_rstd(dve, "n_yb")

            def outb_body(n):
                scaled(group("outb", n), lambda c, w: z_buf[:, c:c + w])
                dve.wait_ge(tile_read, (group("outb", n) + 1).v)
                tt(part(x, n, 0, T), part(x, n, 0, T), z_buf[:, 0:T], add).then_inc(sem("outb_added"), 1)
                dve_operand(dve, "n_ffn0", n, part(x, n, 0, T))
            each(dve, KD, outb_body)

            for layer in range(2):
                if layer:
                    retention_dve(dve, scaled, add_to_x, group)
                    dve.wait_ge(sem("ret_stored"), 1 + 32 * RH)
                name = LAYER[layer]
                dve_rstd(dve, name)
                for q in range(2):
                    nc.vector.memset(gpad[:, q * (T + 4):q * (T + 4) + 2], 0.0)
                off = 0
                for part_, nt in enumerate(FFN_PARTS):
                    gu = f"gu{layer}{part_}"

                    def gate_up(n, off=off, gu=gu):
                        t = n.div(2) + (off + layer * FT)
                        q = n.div(2).mod(2)
                        if n.mod(2) == 0:
                            at = q * (T + 4)
                            if t.k or t.c >= 2:
                                dve.wait_ge(sem("f_silu"), (t + -1).v)
                            scaled(group(gu, n), lambda c, w: gpad[:, at + 2 + c + (2 if c else 0):
                                                                   at + 2 + c + (2 if c else 0) + w],
                                   "f_steps")
                            nc.vector.tensor_copy(gpad[:, at + 2 + TP:at + 4 + TP],
                                                  part(ffn_state, t, 0, 2, 2))\
                                .then_inc(sem("f_steps"), 1)
                            acc = facc[:, q * (T + 2):(q + 1) * (T + 2)]
                            for tap in range(3):
                                dve.wait_ge(sem("f_steps"), (t * 5 + (2 + tap)).v)
                                src = gpad[:, at + tap:at + tap + T + 2]
                                w = col(f"fw{layer}", t + (tap - layer) * FT)
                                if tap == 0:
                                    dve.wait_ge(tile_read, (group(gu, n) + 1).v)
                                    ins = nc.vector.tensor_scalar(acc, src, w, col(f"fb{layer}", t + -layer * FT), mul, add)
                                else:
                                    ins = stt(out=acc, in0=src, scalar=w, in1=acc, op0=mul, op1=add)
                                ins.then_inc(sem("f_steps"), 1)
                        else:
                            h = hid[:, q * T:(q + 1) * T]
                            g_ = group(gu, n)
                            dve.wait_ge(sem("f_scaled"), (t + 1).v)
                            dve.wait_ge(tile_done, (g_ + 1).v)
                            gate = fsgr[:, q * T:(q + 1) * T]
                            tt(two(h[:, 0:TP]), out_prompt(g_), two(gate[:, 0:TP]), mul)
                            tt(h[:, TP:T], out_sample(g_), gate[:, TP:T], mul).then_inc(tile_read, 1)
                            dve.wait_ge(sem("f_hi"), (t + 1).v)
                            tt(part(op_lo[HID[layer]], n.div(2), 0, T), h, part(op_hi[HID[layer]], n.div(2), 0, T), sub)\
                                .then_inc(sem("f_lo"), 1)
                    each(dve, 2 * nt, gate_up, peel=0 if off or layer else 4)
                    down = f"down{layer}{part_}"
                    if part_ < 2:
                        each(dve, KD, lambda n: add_to_x(group(down, n), n))
                    else:
                        dve.wait_ge(sem("p_hi"), layer + 1)
                        tt(op_lo[HID[layer]][:, 6 * T:8 * T], p_raw, op_hi[HID[layer]][:, 6 * T:8 * T], sub)\
                            .then_inc(sem("p_lo"), 1)

                        def last_down(n):
                            add_to_x(group(down, n), n)
                            dve_operand(dve, PLE[layer], n, part(x, n, 0, T))
                        each(dve, KD, last_down)
                    off += nt

                def pp_body(n):
                    for m in range(2):
                        g_ = n * 2 + (PH[f"pp{layer}"].g0 + m)
                        f = n * 2 + m
                        dve.wait_ge(tile_done, (g_ + 1).v)
                        nc.vector.tensor_copy(two(part(p_proj, f, 0, TP)), out_prompt(g_))
                        nc.vector.tensor_copy(part(p_proj, f, TP, TS), out_sample(g_)).then_inc(tile_read, 1)
                each(dve, 4, pp_body)
                dve_rstd(dve, PLE[layer])
                nxt = ("n_mix1", "n_out")[layer]

                def gate_body(n):
                    q = n.mod(2)
                    gt = gate_t[:, q * T:(q + 1) * T]
                    scaled(group(f"gate{layer}", n), lambda c, w: gt[:, c:c + w])
                    dve.wait_ge(sem("g_sig"), (n + (1 + layer * KD)).v)
                    tt(gt, gt, part(p_proj, n, 0, T), mul).then_inc(sem("g_mul"), 1)
                    dve.wait_ge(sem("g_mul"), (n + (1 + layer * KD)).v)
                    tt(part(x, n, 0, T), part(x, n, 0, T), gt, add).then_inc(sem("gate_added"), 1)
                    if layer == 0:
                        dve_operand(dve, nxt, n, part(x, n, 0, T))
                each(dve, KD, gate_body)
            dve_rstd(dve, "n_out")
            for k in range(KD):
                stt(out=part(p_proj, k, 0, T), in0=part(x, k, 0, T), scalar=col("final", k), in1=rstd[:, :],
                    op0=mul, op1=mul).then_inc(sem("y_out"), 1)



def kernel(**inputs):
    import concourse.bacc as bacc
    import concourse.mybir as mybir
    from concourse.bass_utils import run_bass_kernel_spmd

    a = {k: np.asarray(v) for k, v in inputs.items()}

    def tokens(prompt, sample):
        both = np.concatenate([prompt, sample], 0)
        return both.T.reshape(-1, P, T).transpose(1, 0, 2).reshape(P, -1)

    def features(v):
        v = v.reshape(-1, v.shape[-1] // P, P)
        return v.transpose(2, 0, 1).reshape(P, -1)

    def slabs(w, kt, m=1):
        k, f = w.shape
        w = w.reshape(k // (kt * P), kt, P, f // (m * P), m, P)
        return np.ascontiguousarray(w.transpose(0, 3, 2, 1, 4, 5).reshape(-1, P, kt * m * P))

    arrays = {}
    w0, w1 = a["l0_w_in"], a["l1_w_in"]
    arrays["w_u"], arrays["w_v"] = slabs(w0[:, 0:D], 8), slabs(w0[:, D:2 * D], 8)
    arrays["w_z"] = slabs(w0[:, 2 * D:3 * D], 8)
    arrays["w_xbc"] = slabs(w0[:, 3 * D:3 * D + XBC * P], 8)
    arrays["w_dt"] = w0[:, 3 * D + XBC * P:].reshape(KD, P, SH).transpose(1, 0, 2).reshape(P, -1)
    arrays["w_outa"], arrays["w_outb"] = slabs(a["l0_w_out"][0:D], 8), slabs(a["l0_w_out"][D:], 8)
    q, k, v, g = (slabs(w, 8) for w in (w1[:, 0:D], w1[:, D:2 * D], w1[:, 2 * D:4 * D], w1[:, 4 * D:6 * D]))
    heads = np.concatenate([k.reshape(RH, 1, P, -1), q.reshape(RH, 1, P, -1), v.reshape(RH, 2, P, -1),
                            g.reshape(RH, 2, P, -1)], 1)
    arrays["w_heads_a"], arrays["w_heads_b"] = heads[0:5].reshape(30, P, -1), heads[5:8].reshape(18, P, -1)
    arrays["w_ret_a"], arrays["w_ret_b"] = slabs(a["l1_w_out"][0:D], 8), slabs(a["l1_w_out"][D:], 8)
    for layer in range(2):
        off = 0
        for part, nt in enumerate(FFN_PARTS):
            cols = slice(off * P, (off + nt) * P)
            both = np.stack([slabs(a["ffn_w_gate"][layer][:, cols], 8), slabs(a["ffn_w_up"][layer][:, cols], 8)], 1)
            arrays[f"w_gu{layer}{part}"] = both.reshape(2 * nt, P, -1)
            arrays[f"w_down{layer}{part}"] = slabs(a["ffn_w_down"][layer][cols], nt)
            off += nt
        arrays[f"w_pp{layer}"] = slabs(a["ple_w_proj"][layer], 2, 2)
        arrays[f"w_gate{layer}"] = slabs(a["ple_w_gate"][layer], 8)

    f32 = np.float32
    t = np.arange(CH)
    lg = np.log(1.0 - 2.0 ** (-5.0 - np.arange(RH)))
    diff = t[None, :] - t[:, None]
    dmat = np.where(diff[None] >= 0, np.exp(lg[:, None, None] * np.maximum(diff, 0)[None]), 0.0)
    arrays["dmat"] = dmat.transpose(1, 0, 2).reshape(P, -1).astype(f32)
    qdec = np.exp(lg[:, None] * (t + 1.0)).reshape(1, -1)
    arrays["qdec"] = np.broadcast_to(qdec, (P, RH * CH)).astype(f32)
    pos = np.concatenate([np.arange(TP), PAST + np.arange(TS)]).astype(f32)
    inv = f32(10000.0) ** (-np.arange(RDK // 2, dtype=f32) / f32(RDK // 2))
    ang = inv[:, None] * pos[None, :]
    cos, sin = np.cos(ang), np.sin(ang)
    cos, sin = np.concatenate([cos, cos]), np.concatenate([-sin, sin])
    scale = f32(RDK) ** f32(-0.5)
    arrays["cos_q"], arrays["sin_q"] = cos.astype(f32), sin.astype(f32)
    arrays["cos_k"], arrays["sin_k"] = (cos * scale).astype(f32), (sin * scale).astype(f32)
    arrays["ident"] = np.eye(P, dtype=f32)
    arrays["ones"] = np.ones((P, P), f32)
    arrays["tri"] = (t[:, None] <= t[None, :]).astype(f32)
    arrays["neg"] = np.where(t[:, None] <= t[None, :], 0.0, -3e38).astype(f32)
    kdec = np.exp(lg[None, :] * (CH - 1.0 - t)[:, None])
    kdec_s = np.exp(lg[None, :] * (TS - 1.0 - np.minimum(t, TS - 1))[:, None])
    g_chunk = np.broadcast_to(np.exp(lg * CH), (P, RH))
    g_sample = np.broadcast_to(np.exp(lg * TS), (P, RH))

    arrays["vec"] = np.concatenate(
        [features(a[n][layer]) for layer in range(2) for n in ("norm_mix", "norm_ffn", "norm_ple")]
        + [features(a["norm_final"]), features(a["ssm_conv_w"]), features(a["ssm_conv_b"])]
        + [features(a[n][layer]) for layer in range(2) for n in ("ffn_conv_w", "ffn_conv_b")]
        + [features(a["ssm_norm"]), features(a["ret_norm"])]
        + [m.astype(f32) for m in (kdec, kdec_s, g_chunk, g_sample)], 1)
    arrays["x"] = tokens(a["x_prompt"][0], a["x_sample"][0])
    arrays["p"] = np.concatenate([tokens(a["p_prompt"][i, 0], a["p_sample"][i, 0]) for i in range(2)], 1)
    rows = np.concatenate([a["ssm_dt_bias"], a["ssm_a_log"], a["ssm_d"]])
    arrays["head_rows"] = np.broadcast_to(rows[None], (P, 3 * SH))
    arrays["conv_state"] = a["state_ssm_conv"][0].reshape(3, XBC, P).transpose(2, 1, 0).reshape(P, -1)
    arrays["ffn_state"] = a["state_ffn_conv"][:, 0].reshape(2, 2, FT, P).transpose(3, 0, 2, 1).reshape(P, -1)
    arrays["gain_rows"] = np.broadcast_to(a["gm_v_gain"][None], (P, D))
    arrays["w_spatial"] = a["gm_w_s"].transpose(2, 0, 1).reshape(P, -1)
    arrays["bs_row"] = a["gm_b_s"].reshape(1, -1)
    arrays["ssm_state"] = a["state_ssm"][0].reshape(SH * SP_, SN).T
    arrays["ret_state"] = a["state_ret"][0]
    arrays = {n: np.ascontiguousarray(v) for n, v in arrays.items()}

    outs = {"y": (P, KD * T), "conv_tail": (P, XBC * 6), "ssm_prompt": (P, D), "ssm_sample": (P, D),
            "ret_prompt": (RH, RDK, RDV), "ret_sample": (RH, RDK, RDV), "ffn_tail": (P, 2 * FT * 4), "gm_v": (TS, D)}
    nc = bacc.Bacc("TRN2", target_bir_lowering=False, num_devices=1)
    A = {n: nc.dram_tensor("in_" + n, v.shape, mybir.dt.float32, kind="ExternalInput").ap() for n, v in arrays.items()}
    O = {n: nc.dram_tensor("out_" + n, s, mybir.dt.float32, kind="ExternalOutput").ap() for n, s in outs.items()}
    build(nc, A, O)
    r = run_bass_kernel_spmd(nc, [{"in_" + n: v for n, v in arrays.items()}], core_ids=[0]).results[0]
    o = {n: r["out_" + n] for n in outs}

    y = o["y"].reshape(P, KD, T).transpose(2, 1, 0).reshape(T, D)
    tail = o["conv_tail"].reshape(P, XBC, 2, 3).transpose(2, 3, 1, 0).reshape(2, 1, 3, XBC * P)
    ssm = [o[n].T.reshape(1, SH, SP_, SN) for n in ("ssm_prompt", "ssm_sample")]
    ffn = o["ffn_tail"].reshape(P, 2, FT, 2, 2).transpose(3, 1, 4, 2, 0).reshape(2, 2, 1, 2, D_FF)
    c = np.ascontiguousarray
    return (c(y[None, 0:TP]), c(y[None, TP:]), c(tail[0]), c(tail[1]), c(ssm[0]), c(ssm[1]),
            c(o["ret_prompt"][None]), c(o["ret_sample"][None]), c(ffn[0]), c(ffn[1]), c(o["gm_v"][None]))
```
